# Optimizing a Trainium2 kernel written in Bass

```python
import jax, jax.numpy as jnp
from jax import lax
import numpy as np

D_MODEL = 1024
BATCH = 1
SEQ = 1024
DEPTH = 2
DEC_BATCH = 8
DEC_SEQ = 16
PAST_LEN = 256

CHUNK = 64
HEAD_DIM = 64
D_MIX = D_MODEL
D_CONV = D_MIX // 4
CONV_WIDTH = 3
D_ATTN = D_MIX // 2
ATTN_HEADS = D_ATTN // HEAD_DIM
KV_HEADS = 2
GQA_GROUP = ATTN_HEADS // KV_HEADS
D_KV = KV_HEADS * HEAD_DIM
WINDOW = 128
WIN_CHUNKS = WINDOW // CHUNK
ROPE_DIM = HEAD_DIM // 4
ROPE_THETA = 500000.0
D_GMLP = D_MIX // 4
GMLP_HEADS = D_GMLP // HEAD_DIM
GMLP_CHUNK = 128
D_FF = 4 * D_MODEL
D_IN_PROJ = 3 * D_CONV + D_ATTN + 2 * D_KV + 2 * D_GMLP
EPS = 1e-6

kernel_name = "hymba_style_streaming_conv_swa_gmlp"

def rms_norm(x, g):
    xf = x.astype(jnp.float32)
    y = xf * lax.rsqrt(jnp.mean(xf * xf, axis=-1, keepdims=True) + EPS)
    return (y * g.astype(jnp.float32)).astype(x.dtype)

def layer_norm(x, g, b):
    xf = x.astype(jnp.float32)
    mu = jnp.mean(xf, axis=-1, keepdims=True)
    xc = xf - mu
    y = xc * lax.rsqrt(jnp.mean(xc * xc, axis=-1, keepdims=True) + EPS)
    return (y * g.astype(jnp.float32) + b.astype(jnp.float32)).astype(x.dtype)

def partial_rope(x, pos):
    half = ROPE_DIM // 2
    inv_freq = jnp.power(ROPE_THETA, -jnp.arange(half, dtype=jnp.float32) * 2.0 / ROPE_DIM)
    ang = pos.astype(jnp.float32)[:, None] * inv_freq[None, :]
    cos = jnp.cos(ang)[:, None, :].astype(x.dtype)
    sin = jnp.sin(ang)[:, None, :].astype(x.dtype)
    x1, x2, rest = x[..., :half], x[..., half:ROPE_DIM], x[..., ROPE_DIM:]
    return jnp.concatenate([x1 * cos - x2 * sin, x2 * cos + x1 * sin, rest], axis=-1)

def band_mask(q_pos, k_pos):
    qc = q_pos[..., :, None] // CHUNK
    kp = k_pos[..., None, :]
    kc = kp // CHUNK
    return (kp >= 0) & (kc <= qc) & (qc - kc < WIN_CHUNKS)

def sink_softmax(scores, mask, sinks):
    s = jnp.where(mask, scores.astype(jnp.float32), -jnp.inf)
    sink = sinks.astype(jnp.float32).reshape(KV_HEADS, GQA_GROUP)[:, :, None, None]
    m = jnp.maximum(jnp.max(s, axis=-1, keepdims=True), sink)
    e = jnp.exp(s - m)
    return e / (jnp.sum(e, axis=-1, keepdims=True) + jnp.exp(sink - m))

def attn_prompt(q, k, v, sinks):
    B, S = q.shape[:2]
    nc = S // CHUNK
    qb = q.reshape(B, nc, CHUNK, KV_HEADS, GQA_GROUP, HEAD_DIM)
    padw = ((0, 0), ((WIN_CHUNKS - 1) * CHUNK, 0), (0, 0), (0, 0))
    kp = jnp.pad(k, padw).reshape(B, nc + WIN_CHUNKS - 1, CHUNK, KV_HEADS, HEAD_DIM)
    vp = jnp.pad(v, padw).reshape(B, nc + WIN_CHUNKS - 1, CHUNK, KV_HEADS, HEAD_DIM)
    kb = jnp.concatenate([kp[:, j:j + nc] for j in range(WIN_CHUNKS)], axis=2)
    vb = jnp.concatenate([vp[:, j:j + nc] for j in range(WIN_CHUNKS)], axis=2)
    cidx = jnp.arange(nc, dtype=jnp.int32)[:, None]
    q_pos = cidx * CHUNK + jnp.arange(CHUNK, dtype=jnp.int32)[None, :]
    k_pos = (cidx - (WIN_CHUNKS - 1)) * CHUNK + jnp.arange(WIN_CHUNKS * CHUNK, dtype=jnp.int32)[None, :]
    mask = band_mask(q_pos, k_pos)[None, :, None, None]
    scores = jnp.einsum('bcqkgd,bcjkd->bckgqj', qb, kb) * (HEAD_DIM ** -0.5)
    p = sink_softmax(scores, mask, sinks)
    o = jnp.einsum('bckgqj,bcjkd->bcqkgd', p.astype(v.dtype), vb)
    return o.reshape(B, S, D_ATTN)

def attn_sample(q, k_all, v_all, q_pos, k_pos, sinks):
    B, S = q.shape[:2]
    qg = q.reshape(B, S, KV_HEADS, GQA_GROUP, HEAD_DIM)
    scores = jnp.einsum('bqkgd,bjkd->bkgqj', qg, k_all) * (HEAD_DIM ** -0.5)
    p = sink_softmax(scores, band_mask(q_pos, k_pos), sinks)
    o = jnp.einsum('bkgqj,bjkd->bqkgd', p.astype(v_all.dtype), v_all)
    return o.reshape(B, S, D_ATTN)

def short_conv(z, prev, w):
    S = z.shape[1]
    zp = jnp.concatenate([prev, z], axis=1)
    y = w[0] * zp[:, 0:S]
    for j in range(1, CONV_WIDTH):
        y = y + w[j] * zp[:, j:j + S]
    return y, zp[:, S:]

def spatial_gating(u, v_n, w_s, b_s):
    B, S = u.shape[:2]
    nc = -(-S // GMLP_CHUNK)
    vb = jnp.pad(v_n, ((0, 0), (0, nc * GMLP_CHUNK - S), (0, 0)))
    vb = vb.reshape(B, nc, GMLP_CHUNK, GMLP_HEADS, HEAD_DIM)
    blk = jnp.arange(GMLP_CHUNK, dtype=jnp.int32) // CHUNK
    w_m = jnp.where(blk[None, :] <= blk[:, None], w_s, 0)
    mixed = jnp.einsum('gij,bcjgd->bcigd', w_m, vb) + b_s.T[None, None, :, :, None]
    mixed = mixed.reshape(B, nc * GMLP_CHUNK, D_GMLP)[:, :S]
    return u * mixed

def trunk_layer(x, pos, conv_prev, kv_cache, w_norm1, w_in, w_conv, sinks, ln_g, ln_b,
                w_s, b_s, g_grp, w_out, w_norm2, w_ff1, w_ff2):
    B, S = x.shape[:2]
    h = rms_norm(x, w_norm1)
    proj = jnp.einsum('bsd,de->bse', h, w_in)
    splits = [D_CONV, 2 * D_CONV, 3 * D_CONV, 3 * D_CONV + D_ATTN, 3 * D_CONV + D_ATTN + D_KV,
              3 * D_CONV + D_ATTN + 2 * D_KV, 3 * D_CONV + D_ATTN + 2 * D_KV + D_GMLP]
    a, gc, gb, q, k, v, u, vg = jnp.split(proj, splits, axis=-1)
    z, conv_state = short_conv(gc * a, conv_prev, w_conv)
    y_conv = gb * z
    q = partial_rope(q.reshape(B, S, ATTN_HEADS, HEAD_DIM), pos)
    k = partial_rope(k.reshape(B, S, KV_HEADS, HEAD_DIM), pos)
    v = v.reshape(B, S, KV_HEADS, HEAD_DIM)
    if kv_cache is None:
        y_attn = attn_prompt(q, k, v, sinks)
    else:
        k_cache, v_cache = kv_cache
        w_buf = k_cache.shape[1]
        k_pos = jnp.concatenate([PAST_LEN - w_buf + jnp.arange(w_buf, dtype=jnp.int32), pos])
        y_attn = attn_sample(q, jnp.concatenate([k_cache, k], axis=1),
                             jnp.concatenate([v_cache, v], axis=1), pos, k_pos, sinks)
    u = jax.nn.gelu(u, approximate=False)
    vg = layer_norm(jax.nn.gelu(vg, approximate=False), ln_g, ln_b)
    y_gmlp = spatial_gating(u, vg, w_s, b_s)
    mix = jnp.concatenate([rms_norm(y_conv, g_grp[:D_CONV]),
                           rms_norm(y_attn, g_grp[D_CONV:D_CONV + D_ATTN]),
                           rms_norm(y_gmlp, g_grp[D_CONV + D_ATTN:])], axis=-1)
    x = x + jnp.einsum('bse,ed->bsd', mix, w_out)
    h2 = rms_norm(x, w_norm2)
    ff = jnp.square(jax.nn.relu(jnp.einsum('bsd,df->bsf', h2, w_ff1)))
    x = x + jnp.einsum('bsf,fd->bsd', ff, w_ff2)
    return x, conv_state, k, v, vg

def setup_inputs(seed: int = 0) -> dict:
    key = jax.random.key(seed)
    ks = jax.random.split(key, 20)
    f32 = jnp.float32

    def nrm(k, shape, s):
        return jax.random.normal(k, shape, f32) * s

    w_buf = min(WINDOW, PAST_LEN)
    return {
        "x_prompt": nrm(ks[0], (BATCH, SEQ, D_MODEL), 1.0),
        "x_sample": nrm(ks[1], (DEC_BATCH, DEC_SEQ, D_MODEL), 1.0),
        "cache_conv": nrm(ks[2], (DEPTH, DEC_BATCH, CONV_WIDTH - 1, D_CONV), 1.0),
        "cache_k": nrm(ks[3], (DEPTH, DEC_BATCH, w_buf, KV_HEADS, HEAD_DIM), 1.0),
        "cache_v": nrm(ks[4], (DEPTH, DEC_BATCH, w_buf, KV_HEADS, HEAD_DIM), 1.0),
        "w_norm1": 1.0 + nrm(ks[5], (DEPTH, D_MODEL), 0.02),
        "w_in": nrm(ks[6], (DEPTH, D_MODEL, D_IN_PROJ), D_MODEL ** -0.5),
        "w_conv": nrm(ks[7], (DEPTH, CONV_WIDTH, D_CONV), CONV_WIDTH ** -0.5),
        "attn_sinks": nrm(ks[8], (DEPTH, ATTN_HEADS), 1.0),
        "gmlp_ln_g": 1.0 + nrm(ks[9], (DEPTH, D_GMLP), 0.02),
        "gmlp_ln_b": nrm(ks[10], (DEPTH, D_GMLP), 0.02),
        "w_spatial": nrm(ks[11], (DEPTH, GMLP_HEADS, GMLP_CHUNK, GMLP_CHUNK), GMLP_CHUNK ** -0.5),
        "b_spatial": 1.0 + nrm(ks[12], (DEPTH, GMLP_HEADS, GMLP_CHUNK), 0.1),
        "w_group_norm": 1.0 + nrm(ks[13], (DEPTH, D_MIX), 0.02),
        "w_out": nrm(ks[14], (DEPTH, D_MIX, D_MODEL), D_MIX ** -0.5),
        "w_norm2": 1.0 + nrm(ks[15], (DEPTH, D_MODEL), 0.02),
        "w_ff1": nrm(ks[16], (DEPTH, D_MODEL, D_FF), D_MODEL ** -0.5),
        "w_ff2": nrm(ks[17], (DEPTH, D_FF, D_MODEL), D_FF ** -0.5),
        "w_norm_final": 1.0 + nrm(ks[18], (D_MODEL,), 0.02),
    }

def reference(x_prompt, x_sample, cache_conv, cache_k, cache_v, w_norm1, w_in, w_conv, attn_sinks,
              gmlp_ln_g, gmlp_ln_b, w_spatial, b_spatial, w_group_norm, w_out, w_norm2, w_ff1, w_ff2,
              w_norm_final):
    s_p = x_prompt.shape[1]
    s_d = x_sample.shape[1]
    pos_p = jnp.arange(s_p, dtype=jnp.int32)
    pos_d = PAST_LEN + jnp.arange(s_d, dtype=jnp.int32)
    keep = min(WINDOW, s_p)
    xp, xd = x_prompt, x_sample
    conv_p, k_p, v_p, conv_d, k_d, v_d, g_d = [], [], [], [], [], [], []
    for l in range(DEPTH):
        wl = (w_norm1[l], w_in[l], w_conv[l], attn_sinks[l], gmlp_ln_g[l], gmlp_ln_b[l],
              w_spatial[l], b_spatial[l], w_group_norm[l], w_out[l], w_norm2[l], w_ff1[l], w_ff2[l])
        zeros_prev = jnp.zeros((xp.shape[0], CONV_WIDTH - 1, D_CONV), xp.dtype)
        xp, cs, kn, vn, _ = trunk_layer(xp, pos_p, zeros_prev, None, *wl)
        conv_p.append(cs)
        k_p.append(kn[:, s_p - keep:])
        v_p.append(vn[:, s_p - keep:])
        xd, cs, kn, vn, vgn = trunk_layer(xd, pos_d, cache_conv[l], (cache_k[l], cache_v[l]), *wl)
        conv_d.append(cs)
        k_d.append(kn)
        v_d.append(vn)
        g_d.append(vgn)
    y_prompt = rms_norm(xp, w_norm_final)
    y_sample = rms_norm(xd, w_norm_final)
    return (y_prompt, y_sample, jnp.stack(conv_p), jnp.stack(k_p), jnp.stack(v_p),
            jnp.stack(conv_d), jnp.stack(k_d), jnp.stack(v_d), jnp.stack(g_d))


_drawn_inputs = setup_inputs


def setup_inputs(seed=0):
    import zlib

    import numpy as np

    out = dict(_drawn_inputs(seed))
    spreads = {}
    factors = {'attn_sinks': 6.944,
     'gmlp_ln_g': 21.339,
     'gmlp_ln_b': 20.396,
     'w_group_norm': 2.885,
     'w_norm2': 2.678,
     'w_norm_final': 24.488}
    for name, (base, spread) in spreads.items():
        noise = np.random.default_rng([zlib.crc32(name.encode()), seed]).standard_normal(out[name].shape)
        drawn = base * np.exp(spread * noise) if base else spread * noise
        out[name] = __import__('jax').numpy.asarray(drawn.astype(out[name].dtype))
    for name, factor in factors.items():
        out[name] = (out[name] * factor).astype(out[name].dtype)
    return out
```

```python
from contextlib import ExitStack

import numpy as np

import concourse.bass as bass
from concourse import mybir

F32 = mybir.dt.float32
F32R = mybir.dt.float32r
ALU = mybir.AluOpType
ACT = mybir.ActivationFunctionType
AX_X = mybir.AxisListType.X

P = 128
D = 1024
SEQ = 1024
DEPTH = 2
DEC_BATCH = 8
DEC_SEQ = 16
PAST_LEN = 256
CHUNK = 64
HD = 64
HEADS = 8
G4 = 4
D_FF = 4096
ROPE = 16
ROPE_THETA = 500000.0
EPS = 1e-6
T = (SEQ + DEC_BATCH * DEC_SEQ) // P
TS = T - 1
ROWS = T * P
KD = D // P
GROUPS = 3
GW = ROWS // GROUPS
FB = 16
SC = HD ** -0.5
KEYS_S = CHUNK + DEC_SEQ
MASKED = -3.0e38

COL_CONV, COL_Q, COL_KVU, COL_VG = 0, 768, 1280, 1792
U_CONV, U_KVU, U_VG, U_Q, U_OUT, U_FF, U_END = 0, 16, 24, 32, 40, 56, 184
PAD_IDS = range(12, 16)
UNITS = U_END - len(PAD_IDS)
RAW = 4
Y_PER_LAYER = FB * T * 2
H_PER_LAYER = 2 * FB * GROUPS
Y_FULL_PER_LAYER = FB * TS * 2
H_FULL_PER_LAYER = 2 * FB * (GROUPS - 1)


def real(i):
    whole, i = divmod(i, U_END)
    return whole * UNITS + i - len([p for p in PAD_IDS if p < i])


class Signal:

    def __init__(self, nc, ctx, name, plan, now, by=1):
        self.sem = ctx.enter_context(nc.semaphore(name))
        self.plan = plan.setdefault(name, {})
        self.now, self.by, self.n, self.seen = now, by, 0, {}
        plan.setdefault("all", []).append(self)

    def tick(self, key=None):
        self.n += self.by
        self.seen[key] = self.n
        return self.sem, self.by

    def at(self, key):
        n = self.plan.get(key, self.by)
        return self.sem, self.now["l"] * self.plan.get("total", self.by) + n

    def before(self, key):
        return self.sem, self.now["l"] * self.plan.get(key, self.by)


def program(nc, io, plan):
    (x_prompt, x_sample, cache_conv, cache_k, cache_v, w_norm1, w_in, w_conv, sinks, ln_g, ln_b, w_spatial,
     b_spatial, w_group, w_out, w_norm2, w_ff1, w_ff2, w_final, cos_t, sin_t,
     y_prompt, y_sample, conv_p, k_p, v_p, conv_s, k_s, v_s, g_s) = io
    assert DEPTH == 2

    with ExitStack() as ctx:
        cursor = [16512]

        def place(name, shape, dt=F32, at=None):
            size = int(np.prod(shape[1:])) * 4
            if at is None:
                at = cursor[0]
                cursor[0] += (size + 15) // 16 * 16
            return nc.alloc_sbuf_tensor_at(name, shape, dt, offset=at, align_bytes=16)

        x = place("x", [P, T, D])
        hTh = place("hT_hi", [P, KD, ROWS], F32R)
        hTl = place("hT_lo", [P, KD, ROWS], F32R)
        base_u = cursor[0]
        ffh = place("ff_hi", [P, 4, ROWS], F32R)
        ffl = place("ff_lo", [P, 4, ROWS], F32R)
        u_sb = place("u_sb", [P, T, 256], at=base_u)
        kT = place("kT", [P, ROWS], at=base_u + 9216)
        v_sb = place("v_sb", [P, T, P], at=base_u + 13824)
        yc = place("yc", [P, 2, ROWS], at=base_u + 18432)
        base_c = base_u + 27648
        aT = place("aT", [P, ROWS], at=base_c)
        zT = place("zT", [P, 2 + SEQ + DEC_BATCH * (2 + DEC_SEQ)], at=base_c + 4608)
        qn = place("qn", [P, 512], at=base_c)
        qT = place("qT", [P, G4 * P], at=base_c + 2048)
        yat = place("yat", [P, G4, P], at=base_c + 4096)
        sq6 = place("sq6", [P, 6, P], at=base_c + 6144)
        cursor[0] = base_c + 9312
        wh = place("w_hi", [P, 8, 512], F32R)
        wl = place("w_lo", [P, 8, 512], F32R)
        raw = place("w_raw", [P, RAW, 512])
        base_n = cursor[0]
        xn = place("xn", [P, 2, D])
        gN = place("gN", [P, D])
        S = place("S", [P, 2, HEADS * P], at=base_n)
        pT = place("pT", [P, HEADS * P], at=base_n + 8192)
        wnat = place("wnat", [P, 4, P], at=base_n)
        kc = place("kc", [P, 4, P], at=base_n + 2048)
        ccin = place("ccin", [16, 256], at=base_n + 4096)
        cs_out = place("cs_out", [DEC_BATCH, 2, 256], at=base_n + 5120)
        cp_out = place("cp_out", [2, 256], at=base_n + 4096)
        gG = place("gG", [P, 256], at=base_n + 7168)
        kn = place("kn", [P, 2, P], at=base_n + 8192)
        vn = place("vn", [P, 2, 256], at=base_n + 9216)
        yg = place("yg", [P, 256], at=base_n + 11264)
        base_r = cursor[0]
        r_sb = place("r_sb", [P, 2, GW])
        r2_sb = place("r2_sb", [P, 2, GW])
        kcT = place("kcT", [P, 512], at=base_r)
        wsT = place("wsT", [P, 4, P], at=base_r + 2048)
        wsS = place("wsS", [P, 4, P], at=base_r + 4096)
        vs = place("vs", [KEYS_S, DEC_BATCH, P], at=base_r + 2048)
        ident = place("ident", [P, P])
        cosb = place("cosb", [P, T, ROPE])
        sinb = place("sinb", [P, T, ROPE])
        base_l = cursor[0]
        lng = place("lng", [P, 256])
        lnb = place("lnb", [P, 256])
        ycg = place("ycg", [P, 2, P], at=base_l)
        vmix = place("vmix", [P, P], at=base_l + 1024)
        wcT = place("wcT", [P, 2, 3])
        gcT = place("gcT", [P, 6])
        bsp = place("bsp", [P, 2, 4])
        sink = place("sink", [P, 2, HEADS])
        sink1 = place("sink1", [P, 1])
        ccT = place("ccT", [P, 2, 16])
        ones = place("ones", [P, HEADS])
        nhalf = place("nhalf", [P, 4])
        rtA = place("rtA", [P, HEADS, ROPE])
        rtB = place("rtB", [P, HEADS, ROPE])
        ss = place("ss", [P, T])
        ms = place("ms", [P, T])
        rs = place("rs", [P, T])
        bst = place("bst", [P, 6])
        mv = place("mv", [P, 2, 2])
        ve = place("ve", [P, 2])
        rln = place("rln", [P, 2])
        ssG = place("ssG", [P, T])
        sg = place("sg", [P, T, 4])
        rG = place("rG", [P, T, 4])
        mx = place("mx", [P, HEADS])
        sd = place("sd", [P, HEADS])
        es = place("es", [P, HEADS])
        den = place("den", [P, HEADS])
        assert cursor[0] <= 229344, cursor[0]

        ps = ctx.enter_context(nc.psum_tensor("ps", [P, 8, 512], F32))

        now = {"l": 0}

        def sig(name, by=1):
            return Signal(nc, ctx, name, plan, now, by)

        def plain(name):
            return ctx.enter_context(nc.semaphore(name))

        x_in = [plain(f"x_in{t}") for t in range(T)]
        const_in = plain("const_in")
        ident_set = plain("ident_set")
        const_set = plain("const_set")
        raw_in = [plain(f"raw_in{s}") for s in range(RAW)]
        w_hi_done = plain("w_hi_done")
        w_ready = plain("w_ready")
        w_used = plain("w_used")
        h1_full = plain("h1_full")
        relu_done = plain("relu_done")
        r2_done = plain("r2_done")
        ffhi_done = plain("ffhi_done")
        ff_ready = plain("ff_ready")
        y_full = plain("y_full")
        x_added = plain("x_added")
        layer_in = sig("layer_in", 16)
        gn_in = sig("gn_in", 16)
        mid_in = sig("mid_in", 16)
        diag_in = sig("diag_in", 16)
        vs_in = sig("vs_in", 16)
        outs = sig("outs", 16)
        norm_ss, norm_ms, norm_r, xn_ready = sig("norm_ss"), sig("norm_ms"), sig("norm_r"), sig("xn_ready")
        norm_T, norm_hi, norm_lo = sig("norm_T"), sig("norm_hi"), sig("norm_lo")
        conv_full, a_done, z_done, yc_done = sig("conv_full"), sig("a_done"), sig("z_done"), sig("yc_done")
        cc_T, cc_done, zst_T, zst_out = sig("cc_T"), sig("cc_done"), sig("zst_T"), sig("zst_out")
        kvu_full, kn_raw, kvu_done = sig("kvu_full"), sig("kn_raw"), sig("kvu_done")
        k_rot, kT_full, kT_done = sig("k_rot"), sig("kT_full"), sig("kT_done")
        prep_T, ws_done, kc_done, ws_zero = sig("prep_T"), sig("ws_done"), sig("kc_done"), sig("ws_zero")
        vg_full, vg_done, mv_done, ve_done, rln_done = (sig("vg_full"), sig("vg_done"), sig("mv_done"),
                                                        sig("ve_done"), sig("rln_done"))
        vn_ready, mixed_full, y_raw, ssg_done = sig("vn_ready"), sig("mixed_full"), sig("y_raw"), sig("ssg_done")
        yg_ready, ygT_full, ygT_done = sig("yg_ready"), sig("ygT_full"), sig("ygT_done")
        q_full, qn_raw, q_rot, qT_full, qT_done = (sig("q_full"), sig("qn_raw"), sig("q_rot"), sig("qT_full"),
                                                   sig("qT_done"))
        sc_full, s_sub, exp_done, p_ready = sig("sc_full"), sig("s_sub"), sig("exp_done"), sig("p_ready")
        pT_full, pT_act, pT_dve, vmix_set = sig("pT_full"), sig("pT_act"), sig("pT_dve"), sig("vmix_set")
        pv_full, yat_done, sq_done, mix_hi, mix_lo = (sig("pv_full"), sig("yat_done"), sig("sq_done"),
                                                      sig("mix_hi"), sig("mix_lo"))
        ssm_full, sg_done, rg_done = sig("ssm_full"), sig("sg_done"), sig("rg_done")
        out_full, out_acc = sig("out_full"), sig("out_acc")
        dve_step = sig("dve_step")
        fin_in, fin_ss, fin_ms, fin_r, fin_y = [plain(f"fin_{n}") for n in ("in", "ss", "ms", "r", "y")]
        fin_out = [plain(f"fin_out{n}") for n in range(2)]

        block = ctx.enter_context(nc.Block())

        def tile(t):
            return slice(t * P, (t + 1) * P)

        def out_index(n, t, grp):
            return (n * T + t) * 3 + grp

        def y_count(b, t, n):
            return b * 2 * T + 2 * t + n + 1

        def h_count(c, g):
            return c * GROUPS + g + 1

        def slot_free(i, l):
            j = i - 8
            while j in PAD_IDS:
                j -= 8
            return l * real(j + 1 + U_END) if j < 0 else l * UNITS + real(j + 1)

        def released(i):
            return w_used, now["l"] * UNITS + real(i + 1)

        def norm_banks(w, t):
            first = (0, 2)[t % 2] if w == 1 else (3, 5)[t % 2]
            return first, first + 1

        def ids_of_w1(b):
            return U_FF if b == 0 else U_FF + 4 + 8 * (b - 1)

        def ids_of_w2(b):
            return U_FF + 8 + 8 * b if b < FB - 1 else U_END - 4

        @block.sync
        def _(sp):
            for t in range(T):
                src = x_prompt[0, tile(t), :] if t < TS else x_sample.rearrange("b s d -> (b s) d")
                sp.dma_start(x[:, t, :], src).then_inc(x_in[t], 16)

            in_rows = w_in.rearrange("l d e -> (l d) e")
            out_rows = w_out.rearrange("l d e -> (l d) e")
            ff2_rows = w_ff2.rearrange("l d e -> (l d) e")
            in_k = w_in.rearrange("l (k p) e -> (l k) p e", p=P)
            ff1_k = w_ff1.rearrange("l (k p) e -> (l k) p e", p=P)

            def unit(n, shift, halves):
                l, s = now["l"], n % RAW
                if isinstance(shift, int) and n < RAW:
                    sp.wait_ge(w_ready, l * (UNITS + n - RAW + 1))
                else:
                    sp.wait_ge(w_ready, l * UNITS + shift + (n - RAW + 1))
                for dst, src in halves:
                    sp.dma_start(dst, src).then_inc(raw_in[s], 16)

            def rows_unit(n, shift, rows, r0, c0, cols):
                s = n % RAW
                unit(n, shift, [(raw[64 * h:64 * h + 64, s, 0:cols],
                                 rows[bass.ds(r0 + 64 * h, 64), c0:c0 + cols]) for h in range(2)])

            def cols_unit(n, shift, ks, k0, c0):
                s = n % RAW
                dst = raw[:, s, :].rearrange("p (k e) -> p k e", k=4)
                unit(n, shift, [(dst[64 * h:64 * h + 64],
                                 ks[bass.ds(k0, 4), 64 * h:64 * h + 64, bass.ds(c0, P)].rearrange("k p e -> p k e"))
                                for h in range(2)])

            def w1_units(n, shift, f0):
                for c in range(2):
                    for hk in range(2):
                        cols_unit(n + 2 * c + hk, shift, ff1_k, now["l"] * KD + 4 * hk, f0 + c * P)

            def w2_units(n, shift, f0):
                for nh in range(2):
                    for c in range(2):
                        rows_unit(n + 2 * nh + c, shift, ff2_rows, now["l"] * D_FF + f0 + c * P, nh * 512, 512)

            with sp.Fori(0, DEPTH) as l:
                now["l"] = l
                for cb in range(6):
                    col = COL_CONV + (cb % 3) * 256 + (cb // 3) * P
                    for hk in range(2):
                        cols_unit(2 * cb + hk, 0, in_k, l * KD + 4 * hk, col)
                for first, col, cols in ((U_KVU, COL_KVU, 512), (U_VG, COL_VG, 256), (U_Q, COL_Q, 512)):
                    for k in range(KD):
                        rows_unit(real(first + k), 0, in_rows, l * D + k * P, col, cols)
                for n in range(2):
                    for k in range(KD):
                        i = real(U_OUT + n * KD + k)
                        r = [256 + g * 256 + (k - 2) * HD for g in range(2)] if 2 <= k < 6 else [k * P, k * P + 64]
                        unit(i, 0, [(raw[64 * h:64 * h + 64, i % RAW, :],
                                     out_rows[bass.ds(l * D + r[h], 64), n * 512:n * 512 + 512]) for h in range(2)])
                w1_units(real(ids_of_w1(0)), 0, 0)
                with sp.Fori(0, FB - 1) as b:
                    w1_units(real(ids_of_w1(1)), b * 8, b * 256 + 256)
                    w2_units(real(ids_of_w2(0)), b * 8, b * 256)
                w2_units(real(ids_of_w2(FB - 1)), 0, (FB - 1) * 256)
            for t in range(T):
                dst = y_prompt[0, tile(t), :] if t < TS else y_sample.rearrange("b s d -> (b s) d")
                sp.wait_ge(fin_y, t + 1)
                sp.dma_start(dst, xn[:, t % 2, :]).then_inc(fin_out[t % 2], 16)
            sp.wait_ge(fin_out[0], 16 * ((T + 1) // 2))
            sp.wait_ge(fin_out[1], 16 * (T // 2))

        @block.gpsimd
        def _(pool):
            nc.gpsimd.memset(ident[:], 0.0).then_inc(ident_set, 1)
            nc.gpsimd.memset(ones[:], 1.0).then_inc(const_set, 1)
            nc.gpsimd.memset(nhalf[:], -0.5).then_inc(const_set, 1)
            pool.wait_ge(ident_set, 1)
            nc.gpsimd.affine_select(out=ident[:], in_=ident[:], compare_op=ALU.not_equal, fill=1.0, base=0,
                                    pattern=[[-1, P]], channel_multiplier=1).then_inc(ident_set, 1)
            pool.dma_start(cosb[:], cos_t).then_inc(const_in, 16)
            pool.dma_start(sinb[:], sin_t).then_inc(const_in, 16)

            def here():
                pool.nop(nofuse=True)

            def load(dst, src, signal, key=None):
                pool.dma_start(dst, src, allow_slow_non_contiguous=True).then_inc(*signal.tick(key))

            def powers(w):
                for t in range(T):
                    pool.wait_ge(*norm_ss.at((w, t)))
                    here()
                    nc.gpsimd.tensor_scalar(ms[:, t:t + 1], ss[:, t:t + 1], 1.0 / D, EPS, ALU.mult,
                                            ALU.add).then_inc(*norm_ms.tick((w, t)))
                    pool.wait_ge(*norm_ms.at((w, t)))
                    nc.gpsimd.tensor_tensor(rs[:, t:t + 1], ms[:, t:t + 1], nhalf[:, 0:1],
                                            ALU.pow).then_inc(*norm_r.tick((w, t)))

            with pool.Fori(0, DEPTH) as l:
                now["l"] = l
                pool.wait_ge(*xn_ready.before((2, TS)))
                here()
                load(gN[:], w_norm1[bass.ds(l, 1), :].broadcast_to([P, D]), gn_in, 1)
                pool.wait_ge(*mix_lo.before(TS))
                here()
                for c in range(2):
                    load(wcT[:, c, :], w_conv[l, :, c * P:(c + 1) * P].rearrange("j p -> p j"),
                         layer_in)
                    load(gcT[:, c:c + 1], w_group[bass.ds(l, 1), c * P:(c + 1) * P].rearrange("l p -> p l"), layer_in)
                for g in range(2):
                    load(gcT[64 * g:64 * g + 64, 2:6],
                         w_group[bass.ds(l, 1), 256 + 256 * g:512 + 256 * g].rearrange("l (h d) -> d (l h)", d=HD),
                         layer_in)
                load(lng[:], ln_g[bass.ds(l, 1), :].broadcast_to([P, 256]), layer_in)
                load(lnb[:], ln_b[bass.ds(l, 1), :].broadcast_to([P, 256]), layer_in)
                load(bsp[:, 0, :], b_spatial[l].rearrange("g p -> p g"), layer_in)
                load(sink[:, 0, :], sinks[bass.ds(l, 1), :].broadcast_to([P, HEADS]), layer_in)
                for b in range(DEC_BATCH):
                    load(bsp[16 * b:16 * b + 16, 1, :],
                         b_spatial[l, :, 0:16].rearrange("g p -> p g"), layer_in)
                    load(sink1[16 * b:16 * b + 16, :],
                         sinks[bass.ds(l, 1), b:b + 1].broadcast_to([16, 1]), layer_in, "last")
                powers(1)
                pool.wait_ge(*norm_T.at((1, TS)))
                here()
                load(ccin[:], cache_conv[l].rearrange("b j c -> (b j) c"), mid_in)
                load(gG[:], w_group[bass.ds(l, 1), 768:1024].broadcast_to([P, 256]), mid_in)
                load(wnat[:], w_spatial[l].rearrange("g i j -> i g j"), mid_in)
                for b in range(DEC_BATCH):
                    load(kc[64 * (b % 2):64 * (b % 2) + 64, b // 2, :],
                         cache_k[l, b, CHUNK:2 * CHUNK].rearrange("r h d -> r (h d)"), mid_in, "last")
                pool.wait_ge(*zst_out.at(1))
                here()
                load(conv_p[l].rearrange("b j c -> (b j) c"), cp_out[:], outs)
                load(conv_s[l], cs_out[:], outs)
                for t, ko, vo in ((TS - 1, k_p, v_p), (TS, k_s, v_s)):
                    pool.wait_ge(*k_rot.at(t))
                    here()
                    load(ko[l].rearrange("b s h d -> (b s) (h d)"), kn[:, t % 2, :], outs)
                    pool.wait_ge(*kvu_done.at(t))
                    here()
                    load(vo[l].rearrange("b s h d -> (b s) (h d)"), v_sb[:, t, :], outs)
                pool.wait_ge(*ws_done.at("act"))
                pool.wait_ge(*ws_zero.at(None))
                here()
                for b in range(DEC_BATCH):
                    load(wsS[16 * b:16 * b + 16, :, 16 * b:16 * b + 16], wsT[0:16, :, 0:16], diag_in, "last")
                for t in range(T):
                    pool.wait_ge(*mv_done.at(t))
                    here()
                    nc.gpsimd.tensor_scalar(ve[:, t % 2:t % 2 + 1], mv[:, t % 2, 1:2], 1.0, EPS, ALU.mult,
                                            ALU.add).then_inc(*ve_done.tick(t))
                    pool.wait_ge(*ve_done.at(t))
                    nc.gpsimd.tensor_tensor(rln[:, t % 2:t % 2 + 1], ve[:, t % 2:t % 2 + 1], nhalf[:, 0:1],
                                            ALU.pow).then_inc(*rln_done.tick(t))
                pool.wait_ge(*vn_ready.at(TS))
                here()
                load(g_s[l].rearrange("b s c -> (b s) c"), vn[:, TS % 2, :], outs, "last")
                pool.wait_ge(*mixed_full.at(TS))
                here()
                load(vs[0:64], cache_v[l, :, CHUNK:2 * CHUNK].rearrange("b r h d -> r b (h d)"),
                     vs_in)
                for b in range(DEC_BATCH):
                    load(vs[64:80, b, :], v_sb[16 * b:16 * b + 16, TS, :], vs_in, "last")
                for t in range(T):
                    pool.wait_ge(*sg_done.at(t))
                    nc.gpsimd.tensor_tensor(rG[:, t, 0:3], sg[:, t, 0:3], nhalf[:, 0:3],
                                            ALU.pow).then_inc(*rg_done.tick(t))
                pool.wait_ge(*pv_full.at(TS))
                here()
                load(gN[:], w_norm2[bass.ds(l, 1), :].broadcast_to([P, D]), gn_in, 2)
                powers(2)
            now["l"] = DEPTH - 1
            pool.wait_ge(*xn_ready.at((2, TS)))
            pool.dma_start(gN[:], w_final.rearrange("(a d) -> a d", a=1).broadcast_to([P, D])).then_inc(fin_in, 16)
            for t in range(T):
                pool.wait_ge(fin_ss, t + 1)
                nc.gpsimd.tensor_scalar(ms[:, t:t + 1], ss[:, t:t + 1], 1.0 / D, EPS, ALU.mult,
                                        ALU.add).then_inc(fin_ms, 1)
                pool.wait_ge(fin_ms, t + 1)
                nc.gpsimd.tensor_tensor(rs[:, t:t + 1], ms[:, t:t + 1], nhalf[:, 0:1], ALU.pow).then_inc(fin_r, 1)
            pool.wait_ge(*outs.at("last"))

        @block.scalar
        def _(act):
            def split(ids, cols=512):
                for i in ids:
                    l, n = now["l"], real(i)
                    act.wait_ge(raw_in[n % RAW], l * (32 * UNITS // RAW) + 32 * (n // RAW + 1))
                    act.wait_ge(w_used, slot_free(i, l))
                    nc.scalar.activation(wh[:, i % 8, 0:cols], raw[:, n % RAW, 0:cols],
                                         ACT.Copy).then_inc(w_hi_done, 1)

            def split_in_loop(i, it):
                l, n = now["l"], real(i)
                act.wait_ge(raw_in[n % RAW], l * (32 * UNITS // RAW) + it * (32 * 16 // RAW) + 32 * (n // RAW + 1))
                act.wait_ge(w_used, l * UNITS + it * 16 + real(i - 7))
                nc.scalar.activation(wh[:, i % 8, :], raw[:, n % RAW, :], ACT.Copy).then_inc(w_hi_done, 1)

            def norm_sum(w, t):
                if w == 1:
                    act.wait_ge(x_in[t], 16)
                    act.wait_ge(x_added, now["l"] * y_count(FB - 1, t, 1))
                    if t >= 2:
                        act.wait_ge(*norm_T.at((w, t - 2)))
                    else:
                        act.wait_ge(*norm_T.before((2, TS)))
                else:
                    act.wait_ge(*out_acc.at(out_index(1, t, 2)))
                    if t >= 2:
                        act.wait_ge(*norm_T.at((w, t - 2)))
                    else:
                        act.wait_ge(*pT_full.at(TS))
                nc.scalar.activation(xn[:, t % 2, :], x[:, t, :], ACT.Square,
                                     accum_out=ss[:, t:t + 1]).then_inc(*norm_ss.tick((w, t)))

            def norm_high(w, t):
                for h, bank in enumerate(norm_banks(w, t)):
                    act.wait_ge(*norm_T.at((w, t)))
                    nc.scalar.activation(hTh[:, 4 * h:4 * h + 4, tile(t)],
                                         ps[:, bank, :].rearrange("p (k n) -> p k n", k=4),
                                         ACT.Copy).then_inc(*norm_hi.tick((w, t, h)))

            def relu_sq(c, it=0):
                l, bufs, banks = now["l"], c % 4, (3 * (c % 2), 3 * (c % 2) + 1, 3 * (c % 2) + 2)
                cnt = l * H_PER_LAYER + it * (4 * GROUPS)
                full = l * H_FULL_PER_LAYER + it * (4 * (GROUPS - 1))
                used = l * UNITS + it * 16
                for g in range(GROUPS + 1):
                    if g < GROUPS:
                        n = h_count(c, g)
                        if g < GROUPS - 1:
                            act.wait_ge(h1_full, full + c * (GROUPS - 1) + g + 1)
                        else:
                            act.wait_ge(w_used, used + real(ids_of_w1(c // 2) + 2 * (c % 2) + 2))
                        if n > 2:
                            act.wait_ge(r2_done, cnt + n - 2)
                            act.wait_ge(ffhi_done, cnt + n - 2)
                        nc.scalar.activation(r_sb[:, (n - 1) % 2, :], ps[:, banks[g], 0:GW],
                                             ACT.Relu).then_inc(relu_done, 1)
                    if g >= 1:
                        n = h_count(c, g - 1)
                        act.wait_ge(relu_done, cnt + n)
                        nc.scalar.activation(ffh[:, bufs, (g - 1) * GW:g * GW], r_sb[:, (n - 1) % 2, :],
                                             ACT.Square).then_inc(ffhi_done, 1)

            with act.Fori(0, DEPTH) as l:
                now["l"] = l
                for t in range(T + 1):
                    if t < T:
                        norm_sum(1, t)
                    if t >= 1:
                        norm_high(1, t - 1)
                    if t == 3:
                        split(range(U_CONV, U_CONV + 8))
                act.wait_ge(*cc_T.at(None))
                nc.scalar.activation(ccT[:], ps[:, 7, 0:32].rearrange("p (c n) -> p c n", c=2),
                                     ACT.Copy).then_inc(*cc_done.tick())

                def conv_a(c):
                    for g in range(GROUPS):
                        act.wait_ge(*(conv_full.at((3 * c, g)) if g < GROUPS - 1 else released(6 * c + 1)))
                        if c == 1:
                            act.wait_ge(*yc_done.at((0, GROUPS - 1)))
                        nc.scalar.activation(aT[:, g * GW:(g + 1) * GW], ps[:, (4, 0)[(3 * c) % 2] + g, 0:GW],
                                             ACT.Copy).then_inc(*a_done.tick((c, g)))

                def conv_state(c):
                    act.wait_ge(*zst_T.at(c))
                    if c == 0:
                        act.wait_ge(*outs.before("last"))
                    nc.scalar.activation(cp_out[:, c * P:(c + 1) * P], ps[0:2, 7, 0:P], ACT.Copy).then_inc(
                        *zst_out.tick((c, 0)))
                    nc.scalar.activation(cs_out[:, :, c * P:(c + 1) * P],
                                         ps[0:DEC_BATCH, 7, P:3 * P].rearrange("b (j n) -> b j n", j=2), ACT.Copy).then_inc(
                        *zst_out.tick(c))

                conv_a(0)
                split(range(8, 12))
                conv_state(0)
                conv_a(1)
                split(range(U_KVU, U_KVU + 8))
                for t in range(T + 1):
                    if t < T:
                        if t == TS:
                            split(range(U_VG, U_VG + 8), 256)
                        act.wait_ge(*(kvu_full.at(t) if t < TS else released(U_KVU + 7)))
                        if t >= 2:
                            act.wait_ge(*kT_full.at(t - 2))
                        elif t == 0:
                            act.wait_ge(*xn_ready.at((1, TS)))
                        bank = ps[:, 4 + t % 2, :]
                        nc.scalar.activation(kn[:, t % 2, :], bank[:, 0:P], ACT.Copy).then_inc(*kn_raw.tick(t))
                        nc.scalar.activation(v_sb[:, t, :], bank[:, P:2 * P], ACT.Copy).then_inc(
                            *kvu_done.tick((t, "v")))
                        nc.scalar.activation(u_sb[:, t, :], bank[:, 2 * P:512], ACT.Gelu).then_inc(*kvu_done.tick(t))
                    if t == 1:
                        conv_state(1)
                    if t >= 1:
                        act.wait_ge(*kT_full.at(t - 1))
                        nc.scalar.activation(kT[:, tile(t - 1)], ps[:, 6 + (t - 1) % 2, 0:P],
                                             ACT.Copy).then_inc(*kT_done.tick(t - 1))
                for i in range(T + 3):
                    if i < T:
                        if i == TS:
                            split(range(U_Q, U_Q + 8))
                        act.wait_ge(*(vg_full.at(i) if i < TS else released(U_VG + 7)))
                        if i >= 2:
                            act.wait_ge(*mixed_full.at(i - 2))
                        nc.scalar.activation(vn[:, i % 2, :], ps[:, i % 2, 0:256], ACT.Gelu).then_inc(
                            *vg_done.tick(i))
                    if i == 0:
                        act.wait_ge(*prep_T.at("ws"))
                        bank = ps[:, 4, :].rearrange("p (g n) -> p g n", g=4)
                        nc.scalar.activation(wsT[0:64], bank[0:64], ACT.Copy).then_inc(*ws_done.tick("a"))
                        nc.scalar.activation(wsT[64:128, :, 64:128], bank[64:128, :, 64:128],
                                             ACT.Copy).then_inc(*ws_done.tick("act"))
                        act.wait_ge(*prep_T.at("kc"))
                        nc.scalar.activation(kcT[:], ps[:, 5, :], ACT.Copy).then_inc(*kc_done.tick())
                    if 2 <= i < T + 2:
                        t = i - 2
                        act.wait_ge(*y_raw.at(t))
                        nc.scalar.activation(aT[:, 0:256], yg[:], ACT.Square,
                                             accum_out=ssG[:, t:t + 1]).then_inc(*ssg_done.tick(t))
                    if i >= 3:
                        t = i - 3
                        act.wait_ge(*ygT_full.at(t))
                        nc.scalar.activation(u_sb[:, t, :], ps[:, 6 + t % 2, 0:256], ACT.Copy).then_inc(
                            *ygT_done.tick(t))
                for i in range(T + 4):
                    if 1 <= i <= T:
                        t = i - 1
                        act.wait_ge(*qT_full.at(t))
                        if t >= 1:
                            act.wait_ge(*sc_full.at(t - 1))
                        src = ps[:, 2, :]
                        if t < TS:
                            nc.scalar.activation(qT[:], src, ACT.Copy).then_inc(*qT_done.tick(t))
                        else:
                            sv = src.rearrange("p (h b q) -> p b h q", h=G4, b=DEC_BATCH)
                            dv = qT[:].rearrange("p (b h q) -> p b h q", b=DEC_BATCH, h=G4)
                            nc.scalar.activation(dv, sv, ACT.Copy).then_inc(*qT_done.tick(t))
                    if i < T:
                        if i == TS:
                            split(range(U_OUT, U_OUT + 8))
                        act.wait_ge(*(q_full.at(i) if i < TS else released(U_Q + 7)))
                        if i >= 1:
                            act.wait_ge(*qT_full.at(i - 1))
                        else:
                            act.wait_ge(*ssg_done.at(TS))
                        nc.scalar.activation(qn[:].rearrange("p (h g d) -> p g h d", h=G4, g=2),
                                             ps[:, 0, :].rearrange("p (g h d) -> p g h d", g=2, h=G4), ACT.Copy).then_inc(*qn_raw.tick(i))
                    if 1 <= i <= T:
                        t = i - 1
                        w = HEADS * P if t < TS else DEC_BATCH * KEYS_S
                        act.wait_ge(*s_sub.at(t))
                        nc.scalar.activation(S[:, t % 2, 0:w], S[:, t % 2, 0:w], ACT.Exp, scale=SC).then_inc(
                            *exp_done.tick((t, 0)))
                        nc.scalar.activation(es[:], sd[:], ACT.Exp, scale=SC).then_inc(*exp_done.tick(t))
                    if 3 <= i <= T + 2:
                        t = i - 3
                        act.wait_ge(*pv_full.at(t))
                        if t >= 1:
                            act.wait_ge(*ssm_full.at(t - 1))
                        nc.scalar.activation(sq6[:, 0:2, :], yc[:, :, tile(t)], ACT.Square).then_inc(
                            *sq_done.tick((t, 0)))
                        act.wait_ge(*yat_done.at(t))
                        nc.scalar.activation(sq6[:, 2:6, :], ps[:, 7, :].rearrange("p (h n) -> p h n", h=G4),
                                             ACT.Square).then_inc(*sq_done.tick(t))
                        act.wait_ge(*yat_done.at(t))
                        nc.scalar.activation(hTh[:, 0:2, tile(t)], ycg[:], ACT.Copy).then_inc(*mix_hi.tick((t, 0)))
                        nc.scalar.activation(hTh[:, 2:6, tile(t)], yat[:], ACT.Copy).then_inc(*mix_hi.tick((t, 1)))
                        nc.scalar.activation(hTh[:, 6:8, tile(t)],
                                             u_sb[:, t, :].rearrange("p (c n) -> p c n", c=2),
                                             ACT.Copy).then_inc(*mix_hi.tick(t))
                    if 2 <= i <= T + 1:
                        t = i - 2
                        act.wait_ge(*pT_full.at(t))
                        if t >= 1:
                            act.wait_ge(*pv_full.at(t - 1))
                        else:
                            act.wait_ge(*outs.at("last"))
                        n = P if t < TS else KEYS_S
                        nc.scalar.activation(pT[0:n, 0:512], ps[0:n, 5, :], ACT.Copy).then_inc(*pT_act.tick(t))
                split(range(U_OUT + 8, U_OUT + 16))
                for t in range(T + 2):
                    if t == TS:
                        split(range(U_FF, U_FF + 4))
                    if t < T:
                        norm_sum(2, t)
                    if t >= 2:
                        norm_high(2, t - 2)
                split(range(U_FF + 4, U_FF + 8))
                relu_sq(0)
                relu_sq(1)
                with act.Fori(0, (FB - 2) // 2) as it:
                    for b in (1, 2):
                        for i in range(ids_of_w2(b - 1), ids_of_w2(b - 1) + 4):
                            split_in_loop(i, it)
                        relu_sq(2 * b, it)
                        relu_sq(2 * b + 1, it)
                        for i in range(ids_of_w1(b + 1), ids_of_w1(b + 1) + 4):
                            split_in_loop(i, it)
                b = FB - 1
                split(range(ids_of_w2(b - 1), ids_of_w2(b - 1) + 4))
                relu_sq(2 * b)
                relu_sq(2 * b + 1)
                split(range(ids_of_w2(b), ids_of_w2(b) + 4))
            now["l"] = DEPTH - 1
            for t in range(T):
                act.wait_ge(x_added, (DEPTH - 1) * Y_PER_LAYER + y_count(FB - 1, t, 1))
                if t >= 2:
                    act.wait_ge(fin_out[t % 2], 16 * (t // 2))
                else:
                    act.wait_ge(*norm_T.at((2, TS)))
                nc.scalar.activation(xn[:, t % 2, :], x[:, t, :], ACT.Square,
                                     accum_out=ss[:, t:t + 1]).then_inc(fin_ss, 1)

        @block.vector
        def _(dve):
            def link(ins):
                ins.then_inc(*dve_step.tick(dve_step.n))
                dve.wait_ge(*dve_step.at(dve_step.n - 1))

            V = nc.vector

            def lo_unit(n, slot, count, cols=512):
                dve.wait_ge(w_hi_done, count)
                V.tensor_tensor(wl[:, slot, 0:cols], raw[:, n % RAW, 0:cols], wh[:, slot, 0:cols].bitcast(F32),
                                ALU.subtract).then_inc(w_ready, 1)

            def split(ids, cols=512):
                for i in ids:
                    lo_unit(real(i), i % 8, now["l"] * UNITS + real(i) + 1, cols)

            def split_in_loop(i, it):
                lo_unit(real(i), i % 8, now["l"] * UNITS + it * 16 + real(i) + 1)

            def normalise(w, t):
                dve.wait_ge(*norm_r.at((w, t)))
                dve.wait_ge(*gn_in.at(w))
                V.scalar_tensor_tensor(xn[:, t % 2, :], x[:, t, :], rs[:, t:t + 1], gN[:], ALU.mult,
                                       ALU.mult).then_inc(*xn_ready.tick((w, t)))

            def norm_low(w, t):
                for h, bank in enumerate(norm_banks(w, t)):
                    dve.wait_ge(*norm_hi.at((w, t, h)))
                    V.tensor_tensor(hTl[:, 4 * h:4 * h + 4, tile(t)],
                                    ps[:, bank, :].rearrange("p (k n) -> p k n", k=4),
                                    hTh[:, 4 * h:4 * h + 4, tile(t)].bitcast(F32),
                                    ALU.subtract).then_inc(*norm_lo.tick((w, t, h)))

            def rotate(src, heads, t, done):
                v = src.rearrange("p (h d) -> p h d", d=HD)
                c = cosb[:, t, :].unsqueeze(1).broadcast_to([P, heads, ROPE])
                s0 = sinb[:, t, 0:8].unsqueeze(1).broadcast_to([P, heads, 8])
                s1 = sinb[:, t, 8:16].unsqueeze(1).broadcast_to([P, heads, 8])
                V.tensor_tensor(rtA[:, 0:heads, :], v[:, :, 0:16], c, ALU.mult)
                V.tensor_tensor(rtB[:, 0:heads, 0:8], v[:, :, 8:16], s0, ALU.mult)
                link(V.tensor_tensor(rtB[:, 0:heads, 8:16], v[:, :, 0:8], s1, ALU.mult))
                V.tensor_tensor(v[:, :, 0:16], rtA[:, 0:heads, :], rtB[:, 0:heads, :], ALU.add).then_inc(*done.tick(t))
                dve.wait_ge(*done.at(t))

            zs = zT[:, 2 + SEQ:].rearrange("p (b n) -> p b n", b=DEC_BATCH)

            def conv_z(c):
                dve.wait_ge(*cc_done.at(None))
                if c == 0:
                    dve.wait_ge(*conv_full.at((1, 0)))
                    V.memset(zT[:, 0:2], 0.0)
                else:
                    dve.wait_ge(*zst_T.at(0))
                V.tensor_copy(zs[:, :, 0:2], ccT[:, c, :].rearrange("p (b j) -> p b j", j=2))
                for g in range(GROUPS):
                    cb = 3 * c + 1
                    bank = ps[:, (4, 0)[cb % 2] + g, :]
                    dve.wait_ge(*(conv_full.at((cb, g)) if g < GROUPS - 1 else released(2 * cb + 1)))
                    dve.wait_ge(*a_done.at((c, g)))
                    n = GW if g < GROUPS - 1 else SEQ - g * GW
                    last = V.tensor_tensor(zT[:, 2 + g * GW:2 + g * GW + n], bank[:, 0:n],
                                           aT[:, g * GW:g * GW + n], ALU.mult)
                    if g == GROUPS - 1:
                        last = V.tensor_tensor(zs[:, :, 2:], bank[:, n:GW].rearrange("p (b q) -> p b q", b=DEC_BATCH),
                                               aT[:, SEQ:].rearrange("p (b q) -> p b q", b=DEC_BATCH), ALU.mult)
                    last.then_inc(*z_done.tick((c, g)))

            def conv_taps(c):
                dve.wait_ge(*z_done.at((c, GROUPS - 1)))
                dve.wait_ge(*layer_in.at("last"))
                for zv, yv in ((lambda j: zT[:, j:j + SEQ], aT[:, 0:SEQ]),
                               (lambda j: zs[:, :, j:j + DEC_SEQ],
                                aT[:, SEQ:].rearrange("p (b q) -> p b q", b=DEC_BATCH))):
                    link(V.tensor_scalar(yv, zv(0), wcT[:, c, 0:1], None, ALU.mult))
                    for j in (1, 2):
                        link(V.scalar_tensor_tensor(yv, zv(j), wcT[:, c, j:j + 1], yv, ALU.mult, ALU.add))

            def conv_gate(c):
                for g in range(GROUPS):
                    cb = 3 * c + 2
                    dve.wait_ge(*(conv_full.at((cb, g)) if g < GROUPS - 1 else released(2 * cb + 1)))
                    V.tensor_tensor(yc[:, c, g * GW:(g + 1) * GW], ps[:, (4, 0)[cb % 2] + g, 0:GW],
                                    aT[:, g * GW:(g + 1) * GW], ALU.mult).then_inc(*yc_done.tick((c, g)))

            def scores_view(t):
                w = P if t < TS else KEYS_S
                return ps[:, 3:5, 0:4 * w].rearrange("p b (h n) -> p b h n", h=4), w

            def s_view(t, w):
                return S[:, t % 2, 0:8 * w].rearrange("p (b h n) -> p b h n", b=2, h=4)

            def by_head(v, w):
                return v.rearrange("p (b h) -> p b h", b=2).unsqueeze(3).broadcast_to([P, 2, 4, w])

            def softmax_max(t):
                v, w = scores_view(t)
                dve.wait_ge(*sc_full.at(t))
                if t == 0:
                    link(V.memset(ps[0:64, 3:5, :].rearrange("p b (h n) -> p (b h) n", h=4)[:, :, CHUNK:P], MASKED))
                kind = 0 if t < TS else 1
                link(V.tensor_reduce(mx[:].rearrange("p (b h) -> p b h", b=2), v, AX_X, ALU.max))
                link(V.tensor_tensor(mx[:], mx[:], sink[:, kind, :], ALU.max))
                if t >= 2:
                    dve.wait_ge(*pT_full.at(t - 2))
                V.tensor_tensor(s_view(t, w), v, by_head(mx[:], w), ALU.subtract)
                V.tensor_tensor(sd[:], sink[:, kind, :], mx[:], ALU.subtract).then_inc(*s_sub.tick(t))

            def softmax_norm(t):
                w = P if t < TS else KEYS_S
                dve.wait_ge(*exp_done.at(t))
                link(V.tensor_reduce(den[:].rearrange("p (b h) -> p b h", b=2), s_view(t, w), AX_X, ALU.add))
                link(V.tensor_tensor(den[:], den[:], es[:], ALU.add))
                link(V.reciprocal(den[:], den[:]))
                V.tensor_tensor(s_view(t, w), s_view(t, w), by_head(den[:], w), ALU.mult).then_inc(*p_ready.tick(t))

            def mixed_rows(t):
                dve.wait_ge(*pv_full.at(t))
                if t >= 1:
                    dve.wait_ge(*mix_hi.at(t - 1))
                V.tensor_tensor(yat[:], ps[:, 7, :].rearrange("p (h n) -> p h n", h=G4),
                                gcT[:, 2:6].unsqueeze(2).broadcast_to([P, G4, P]), ALU.mult)
                V.tensor_tensor(ycg[:], yc[:, :, tile(t)], gcT[:, 0:2].unsqueeze(2).broadcast_to([P, 2, P]),
                                ALU.mult).then_inc(*yat_done.tick(t))

            def mixed_low(t):
                dve.wait_ge(*mix_hi.at(t))
                for k0, k1, src in ((0, 2, ycg[:]), (2, 6, yat[:]),
                                    (6, 8, u_sb[:, t, :].rearrange("p (c n) -> p c n", c=2))):
                    last = V.tensor_tensor(hTl[:, k0:k1, tile(t)], src, hTh[:, k0:k1, tile(t)].bitcast(F32),
                                           ALU.subtract)
                last.then_inc(*mix_lo.tick(t))

            def project_out(n, t):
                for grp in range(3):
                    q = out_index(n, t, grp)
                    unit = U_OUT + 8 * n + (1, 5, 7)[grp]
                    if n == 0 and t == TS:
                        split(range(U_OUT + 8 + (0, 2, 6)[grp], U_OUT + 8 + (2, 6, 8)[grp]))
                    dve.wait_ge(*(out_full.at(q) if t < TS else released(unit)))
                    dve.wait_ge(*rg_done.at(t))
                    if q >= 1:
                        dve.wait_ge(*out_acc.at(q - 1))
                    V.scalar_tensor_tensor(x[:, t, n * 512:n * 512 + 512], ps[:, (0, 2)[q % 2], :],
                                           rG[:, t, grp:grp + 1], x[:, t, n * 512:n * 512 + 512], ALU.mult,
                                           ALU.add).then_inc(*out_acc.tick(q))

            def square_low(c, it=0):
                cnt = now["l"] * H_PER_LAYER + it * (4 * GROUPS)
                for g in range(GROUPS + 1):
                    if g < GROUPS:
                        n = h_count(c, g)
                        dve.wait_ge(relu_done, cnt + n)
                        if n > 2:
                            dve.wait_ge(ff_ready, cnt + n - 2)
                        V.tensor_tensor(r2_sb[:, (n - 1) % 2, :], r_sb[:, (n - 1) % 2, :], r_sb[:, (n - 1) % 2, :],
                                        ALU.mult).then_inc(r2_done, 1)
                    if g >= 1:
                        n = h_count(c, g - 1)
                        dve.wait_ge(ffhi_done, cnt + n)
                        dve.wait_ge(r2_done, cnt + n)
                        V.tensor_tensor(ffl[:, c % 4, (g - 1) * GW:g * GW], r2_sb[:, (n - 1) % 2, :],
                                        ffh[:, c % 4, (g - 1) * GW:g * GW].bitcast(F32),
                                        ALU.subtract).then_inc(ff_ready, 1)

            def add_ff2(b, it=0, ids=(), looped=False):
                l = now["l"]
                for t in range(T):
                    for n in range(2):
                        cnt = l * Y_PER_LAYER + it * (4 * T) + y_count(b, t, n)
                        if t < TS:
                            dve.wait_ge(y_full, l * Y_FULL_PER_LAYER + it * (4 * TS) + b * 2 * TS + 2 * t + n + 1)
                        else:
                            dve.wait_ge(w_used, l * UNITS + it * 16 + real(ids_of_w2(b) + 2 * n + 2))
                        if b >= 1:
                            dve.wait_ge(x_added, cnt - 2 * T)
                        xv = x[:, t, n * 512:n * 512 + 512]
                        V.tensor_tensor(xv, ps[:, 6 + n, :], xv, ALU.add).then_inc(x_added, 1)
                    if t < len(ids):
                        split_in_loop(ids[t], it) if looped else split([ids[t]])

            dve.wait_ge(const_in, 32)
            dve.wait_ge(const_set, 2)
            with dve.Fori(0, DEPTH) as l:
                now["l"] = l
                for t in range(T + 1):
                    if t < T:
                        normalise(1, t)
                    if t >= 1:
                        norm_low(1, t - 1)
                    if t == 3:
                        split(range(U_CONV, U_CONV + 8))
                conv_z(0)
                split(range(8, 12))
                conv_taps(0)
                conv_gate(0)
                conv_z(1)
                conv_taps(1)
                split(range(U_KVU, U_KVU + 8))
                conv_gate(1)
                for t in range(T):
                    if t == TS:
                        split(range(U_VG, U_VG + 8), 256)
                    dve.wait_ge(*kn_raw.at(t))
                    rotate(kn[:, t % 2, :], 2, t, k_rot)
                V.memset(wsT[64:128, :, 0:64], 0.0)
                V.memset(wsS[:], 0.0).then_inc(*ws_zero.tick())
                for i in range(T + 2):
                    if i < T:
                        if i == TS:
                            split(range(U_Q, U_Q + 8))
                        dve.wait_ge(*vg_done.at(i))
                        link(V.bn_stats(bst[:], vn[:, i % 2, :]))
                        dve.nop(nofuse=True)
                        V.bn_aggr(mv[:, i % 2, :], bst[:]).then_inc(*mv_done.tick(i))
                        dve.wait_ge(*mv_done.at(i))
                    if 1 <= i <= T:
                        t = i - 1
                        row = vn[:, t % 2, :]
                        dve.wait_ge(*rln_done.at(t))
                        link(V.tensor_scalar(row, row, mv[:, t % 2, 0:1], rln[:, t % 2:t % 2 + 1], ALU.subtract,
                                             ALU.mult))
                        link(V.tensor_tensor(row, row, lng[:], ALU.mult))
                        V.tensor_tensor(row, row, lnb[:], ALU.add).then_inc(*vn_ready.tick(t))
                    if i >= 2:
                        t = i - 2
                        kind = 0 if t < TS else 1
                        dve.wait_ge(*mixed_full.at(t))
                        if t >= 1:
                            dve.wait_ge(*ssg_done.at(t - 1))
                            dve.wait_ge(*yg_ready.at(t - 1))
                        link(V.tensor_tensor(yg[:].rearrange("p (g d) -> p g d", g=4),
                                             ps[:, 2 + t % 2, 0:256].rearrange("p (g d) -> p g d", g=4),
                                             bsp[:, kind, :].unsqueeze(2).broadcast_to([P, 4, HD]), ALU.add))
                        V.tensor_tensor(yg[:], yg[:], u_sb[:, t, :], ALU.mult).then_inc(*y_raw.tick(t))
                        dve.wait_ge(*y_raw.at(t))
                        V.tensor_tensor(u_sb[:, t, :], yg[:], gG[:], ALU.mult).then_inc(*yg_ready.tick(t))
                V.tensor_scalar(sink[:, 1, :], ones[:], sink1[:, 0:1], 8.0, ALU.mult, ALU.mult)
                link(V.tensor_scalar(sink[:, 0, :], sink[:, 0, :], 8.0, None, ALU.mult))
                for i in range(T + 4):
                    if i < T:
                        if i == TS:
                            split(range(U_OUT, U_OUT + 8))
                        dve.wait_ge(*qn_raw.at(i))
                        rotate(qn[:], HEADS, i, q_rot)
                    if 1 <= i <= T:
                        softmax_max(i - 1)
                    if 3 <= i <= T + 2:
                        mixed_rows(i - 3)
                    if 2 <= i <= T + 1:
                        t = i - 2
                        n = P if t < TS else KEYS_S
                        dve.wait_ge(*pT_full.at(t))
                        if t >= 1:
                            dve.wait_ge(*pv_full.at(t - 1))
                        if t < TS:
                            V.tensor_copy(vmix[0:64, :], v_sb[0:64, t, :])
                            if t == 0:
                                V.memset(vmix[64:128, :], 0.0)
                            else:
                                V.tensor_copy(vmix[64:128, :], v_sb[64:128, t - 1, :])
                        V.tensor_copy(pT[0:n, 512:1024], ps[0:n, 6, :]).then_inc(*pT_dve.tick(t))
                    if 1 <= i <= T:
                        softmax_norm(i - 1)
                    if 3 <= i <= T + 2:
                        mixed_low(i - 3)
                    if i >= 4:
                        t = i - 4
                        dve.wait_ge(*ssm_full.at(t))
                        V.tensor_scalar(sg[:, t, 0:1], ps[:, 1, 0:1], 1.0 / 256, EPS, ALU.mult, ALU.add)
                        V.tensor_scalar(sg[:, t, 1:2], ps[:, 1, 1:2], 1.0 / 512, EPS, ALU.mult, ALU.add)
                        V.tensor_scalar(sg[:, t, 2:3], ssG[:, t:t + 1], 1.0 / 256, EPS, ALU.mult,
                                        ALU.add).then_inc(*sg_done.tick(t))
                    if i >= T:
                        project_out(0, i - T)
                for t in range(4, T):
                    project_out(0, t)
                for t in range(T + 2):
                    if t == TS:
                        split(range(U_FF, U_FF + 4))
                    if t < T:
                        project_out(1, t)
                    if 1 <= t <= T:
                        normalise(2, t - 1)
                    if t >= 2:
                        norm_low(2, t - 2)
                split(range(U_FF + 4, U_FF + 8))
                square_low(0)
                square_low(1)

                def block_of_ff(b, it=0, looped=False, ids=()):
                    for i in range(ids_of_w2(b - 1), ids_of_w2(b - 1) + 4):
                        split_in_loop(i, it) if looped else split([i])
                    square_low(2 * b, it)
                    square_low(2 * b + 1, it)
                    add_ff2(b - 1, it, ids, looped)

                dve.wait_ge(*out_acc.at(out_index(1, TS, 2)))
                dve.nop(nofuse=True)
                with dve.Fori(0, (FB - 2) // 2) as it:
                    for b in (1, 2):
                        block_of_ff(b, it, True, range(ids_of_w1(b + 1), ids_of_w1(b + 1) + 4))
                block_of_ff(FB - 1, ids=range(ids_of_w2(FB - 1), ids_of_w2(FB - 1) + 4))
                add_ff2(FB - 1)
            dve.wait_ge(fin_in, 16)
            for t in range(T):
                dve.wait_ge(fin_r, t + 1)
                V.scalar_tensor_tensor(xn[:, t % 2, :], x[:, t, :], rs[:, t:t + 1], gN[:], ALU.mult,
                                       ALU.mult).then_inc(fin_y, 1)

        @block.tensor
        def _(pe):
            def product(out, sh, sl, mh, ml, first, last):
                pe.matmul(out, sh, mh, start=first, stop=False)
                pe.matmul(out, sh, ml, start=False, stop=False)
                return pe.matmul(out, sl, mh, start=False, stop=last)

            def unit_ready(i):
                pe.wait_ge(w_ready, now["l"] * UNITS + real(i) + 1)

            def rows_by_cols(out, t, first_id, ks, cols=512):
                for k in ks:
                    if t == 0:
                        unit_ready(first_id + k)
                    s = (first_id + k) % 8
                    ins = product(out, hTh[:, k, tile(t)], hTl[:, k, tile(t)], wh[:, s, 0:cols], wl[:, s, 0:cols],
                                  k == ks[0], k == ks[-1])
                    if t == TS:
                        ins.then_inc(w_used, 1)
                return ins

            def cols_by_rows(out, g, first_id, it=0, check=True):
                for k in range(KD):
                    i = first_id + k // 4
                    if g == 0 and k % 4 == 0:
                        pe.wait_ge(w_ready, now["l"] * UNITS + it * 16 + real(i) + 1)
                    w0 = (k % 4) * P
                    ins = product(out, wh[:, i % 8, w0:w0 + P], wl[:, i % 8, w0:w0 + P],
                                  hTh[:, k, g * GW:(g + 1) * GW], hTl[:, k, g * GW:(g + 1) * GW],
                                  k == 0, k == KD - 1)
                    if g == GROUPS - 1 and k % 4 == 3:
                        ins.then_inc(w_used, 1)
                return ins

            def norm_turn(w, t):
                pe.wait_ge(*xn_ready.at((w, t)))
                if t >= 2:
                    pe.wait_ge(*norm_lo.at((w, t - 2, 1)))
                for k in range(KD):
                    bank = norm_banks(w, t)[k // 4]
                    ins = pe.transpose(ps[:, bank, (k % 4) * P:(k % 4 + 1) * P], xn[:, t % 2, tile(k)], ident[:])
                ins.then_inc(*norm_T.tick((w, t)))

            def conv_cols(cb, g):
                if cb >= 2:
                    c, kind = divmod(cb - 2, 3)
                    pe.wait_ge(*(a_done, z_done, yc_done)[kind].at((c, g)))
                elif cb == 1:
                    pe.wait_ge(*norm_lo.at((1, TS, 1)))
                    pe.wait_ge(*norm_lo.at((1, TS - 1, 1)))
                else:
                    pe.wait_ge(*norm_lo.at((1, 3 * g + 2, 1)))
                ins = cols_by_rows(ps[:, (4, 0)[cb % 2] + g, 0:GW], g, 2 * cb)
                if g < GROUPS - 1:
                    ins.then_inc(*conv_full.tick((cb, g)))

            def conv_state(c):
                pe.wait_ge(*z_done.at((c, GROUPS - 1)))
                if c == 0:
                    pe.wait_ge(*cc_done.at(None))
                else:
                    pe.wait_ge(*zst_out.at(0))
                pe.transpose(ps[0:2, 7, 0:P], zT[:, SEQ:SEQ + 2], ident[:])
                z_streams = zT[:, 2 + SEQ:].rearrange("p (b n) -> p b n", b=DEC_BATCH)
                for j in range(2):
                    ins = pe.transpose(ps[0:DEC_BATCH, 7, (1 + j) * P:(2 + j) * P], z_streams[:, :, DEC_SEQ + j],
                                       ident[:])
                ins.then_inc(*zst_T.tick(c))

            def spatial_mix(t):
                w = wsT if t < TS else wsS
                if t == 0:
                    pe.wait_ge(*ws_done.at("act"))
                    pe.wait_ge(*ws_zero.at(None))
                    pe.wait_ge(*yc_done.at((1, 2)))
                if t == TS:
                    pe.wait_ge(*diag_in.at("last"))
                pe.wait_ge(*vn_ready.at(t))
                if t >= 2:
                    pe.wait_ge(*yg_ready.at(t - 2))
                for g in range(4):
                    ins = pe.matmul(ps[:, 2 + t % 2, g * HD:(g + 1) * HD], w[:, g, :], vn[:, t % 2, g * HD:(g + 1) * HD],
                                    start=True, stop=True)
                ins.then_inc(*mixed_full.tick(t))

            def gated_turn(t):
                pe.wait_ge(*yg_ready.at(t))
                pe.wait_ge(*(ygT_done.at(t - 2) if t >= 2 else kT_done.at(TS - t)))
                pe.transpose(ps[:, 6 + t % 2, 0:P], u_sb[:, t, 0:P], ident[:])
                pe.transpose(ps[:, 6 + t % 2, P:2 * P], u_sb[:, t, P:2 * P], ident[:]).then_inc(*ygT_full.tick(t))

            def q_turn(t):
                pe.wait_ge(*q_rot.at(t))
                if t >= 1:
                    pe.wait_ge(*qT_done.at(t - 1))
                for h in range(G4):
                    ins = pe.transpose(ps[:, 2, h * P:(h + 1) * P], qn[:, h * P:(h + 1) * P], ident[:])
                ins.then_inc(*qT_full.tick(t))

            def scores(t):
                pe.wait_ge(*qT_done.at(t))
                if t >= 1:
                    pe.wait_ge(*s_sub.at(t - 1))
                else:
                    pe.wait_ge(*kT_done.at(TS))
                    pe.wait_ge(*kc_done.at(None))
                pe.nop(nofuse=True)
                k0 = t * P
                for g in range(2):
                    rows = slice(64 * g, 64 * g + 64)
                    bank = ps[:, 3 + g, :]
                    for h in range(G4):
                        if t == TS:
                            break
                        c0 = h * P
                        qh = qT[rows, h * P:(h + 1) * P]
                        pe.matmul(bank[0:64, c0:c0 + 64], qh[:, 0:64], kT[rows, k0:k0 + 64], start=True, stop=True)
                        if t > 0:
                            pe.matmul(bank[0:64, c0 + 64:c0 + P], qh[:, 0:64], kT[rows, k0 - 64:k0], start=True,
                                      stop=True)
                        ins = pe.matmul(bank[64:128, c0:c0 + P], qh[:, 64:128], kT[rows, k0:k0 + P], start=True,
                                        stop=True)
                if t == TS:
                    for b in range(DEC_BATCH):
                        bank = ps[:, 3 + b // 4, (b % 4) * KEYS_S:(b % 4 + 1) * KEYS_S]
                        for g in range(2):
                            rows = slice(64 * g, 64 * g + 64)
                            qb = qT[rows, b * 64:(b + 1) * 64]
                            pe.matmul(bank[rows, 0:64], qb, kcT[rows, b * 64:(b + 1) * 64], start=True, stop=True)
                            ins = pe.matmul(bank[rows, 64:80], qb, kT[rows, k0 + 16 * b:k0 + 16 * b + 16],
                                            start=True, stop=True)
                ins.then_inc(*sc_full.tick(t))

            def p_turn(t):
                pe.wait_ge(*p_ready.at(t))
                if t >= 1:
                    pe.wait_ge(*pT_act.at(t - 1))
                    pe.wait_ge(*pT_dve.at(t - 1))
                n = P if t < TS else KEYS_S
                for h in range(HEADS):
                    ins = pe.transpose(ps[0:n, 5 + h // 4, (h % 4) * P:(h % 4 + 1) * P],
                                       S[:, t % 2, h * n:(h + 1) * n], ident[:])
                ins.then_inc(*pT_full.tick(t))

            def values(t):
                pe.wait_ge(*pT_act.at(t))
                pe.wait_ge(*pT_dve.at(t))
                if t >= 1:
                    pe.wait_ge(*sq_done.at(t - 1))
                else:
                    pe.wait_ge(*ygT_done.at(TS - 1))
                out = ps[:, 7, :].rearrange("p (h n) -> p h n", h=G4)
                pv = pT[:].rearrange("p (g h n) -> p g h n", g=2, h=G4)
                if t < TS:
                    for g in range(2):
                        rows = slice(64 * g, 64 * g + 64)
                        for half, vv in enumerate((vmix[:, rows], v_sb[:, t, rows])):
                            q = slice(64 * half, 64 * half + 64)
                            ins = pe.matmul(out[rows, :, q], vv, pv[:, g, :, q], start=True, stop=True)
                else:
                    pe.wait_ge(*vs_in.at("last"))
                    for b in range(DEC_BATCH):
                        for g in range(2):
                            rows = slice(64 * g, 64 * g + 64)
                            ins = pe.matmul(out[rows, :, 16 * b:16 * b + 16], vs[0:KEYS_S, b, rows],
                                            pT[0:KEYS_S, b * P + 64 * g:b * P + 64 * g + 64], start=True, stop=True)
                ins.then_inc(*pv_full.tick(t))

            def group_sums(t):
                pe.wait_ge(*sq_done.at(t))
                if t >= 1:
                    pe.wait_ge(*sg_done.at(t - 1))
                for col, ks in ((0, range(0, 2)), (1, range(2, 6))):
                    for k in ks:
                        ins = pe.matmul(ps[:, 1, col:col + 1], sq6[:, k, :], ones[:, 0:1], start=k == ks[0],
                                        stop=k == ks[-1])
                ins.then_inc(*ssm_full.tick(t))

            def project_out(n, t):
                for grp, ks in enumerate((range(0, 2), range(2, 6), range(6, 8))):
                    q = out_index(n, t, grp)
                    if grp == 0 and n == 0:
                        pe.wait_ge(*mix_lo.at(t))
                    if q >= 2:
                        pe.wait_ge(*out_acc.at(q - 2))
                    else:
                        pe.wait_ge(*(qn_raw, qT_done)[q].at(TS))
                    ins = rows_by_cols(ps[:, (0, 2)[q % 2], :], t, U_OUT + 8 * n, list(ks))
                    if t < TS:
                        ins.then_inc(*out_full.tick(q))

            def ff1(b, it=0, groups=range(GROUPS), chunks=(0, 1)):
                l = now["l"]
                for cc in chunks:
                    c = 2 * b + cc
                    for g in groups:
                        if c >= 2:
                            pe.wait_ge(relu_done, l * H_PER_LAYER + it * (4 * GROUPS) + h_count(c - 2, g))
                        ins = cols_by_rows(ps[:, 3 * cc + g, 0:GW], g, ids_of_w1(b) + 2 * cc, it)
                        if g < GROUPS - 1:
                            ins.then_inc(h1_full, 1)

            def ff2(b, it=0):
                l = now["l"]
                for t in range(T):
                    if t % 3 == 0:
                        pe.wait_ge(ff_ready, l * H_PER_LAYER + it * (4 * GROUPS) + h_count(2 * b + 1, t // 3))
                    for n in range(2):
                        if b > 0 or t > 0:
                            pe.wait_ge(x_added, l * Y_PER_LAYER + it * (4 * T) + y_count(b, t, n) - 2)
                        for cc in range(2):
                            i = ids_of_w2(b) + 2 * n + cc
                            if t == 0:
                                pe.wait_ge(w_ready, l * UNITS + it * 16 + real(i) + 1)
                            ch = (2 * b + cc) % 4
                            ins = product(ps[:, 6 + n, :], ffh[:, ch, tile(t)], ffl[:, ch, tile(t)], wh[:, i % 8, :],
                                          wl[:, i % 8, :], cc == 0, cc == 1)
                            if t == TS:
                                ins.then_inc(w_used, 1)
                        if t < TS:
                            ins.then_inc(y_full, 1)

            pe.wait_ge(ident_set, 2)
            pe.wait_ge(const_set, 2)
            with pe.Fori(0, DEPTH) as l:
                now["l"] = l
                pe.wait_ge(relu_done, l * H_PER_LAYER)
                pe.wait_ge(x_added, l * Y_PER_LAYER)
                for g in range(GROUPS):
                    for t in range(3 * g, 3 * g + 3):
                        norm_turn(1, t)
                    conv_cols(0, g)
                pe.wait_ge(*mid_in.at("last"))
                pe.nop(nofuse=True)
                for c in range(2):
                    ins = pe.transpose(ps[:, 7, 16 * c:16 * c + 16], ccin[0:16, c * P:(c + 1) * P], ident[0:16, 0:16])
                ins.then_inc(*cc_T.tick())
                for cb in range(1, 6):
                    for g in range(GROUPS):
                        conv_cols(cb, g)
                    if cb == 2:
                        conv_state(0)
                for t in range(T + 1):
                    if t < T:
                        pe.wait_ge(*(kvu_done.at(t - 2) if t >= 2 else z_done.at((1, t))))
                        ins = rows_by_cols(ps[:, 4 + t % 2, :], t, U_KVU, list(range(KD)))
                        if t < TS:
                            ins.then_inc(*kvu_full.tick(t))
                    if t == 1:
                        conv_state(1)
                    if t >= 1:
                        pe.wait_ge(*k_rot.at(t - 1))
                        if t - 1 >= 2:
                            pe.wait_ge(*kT_done.at(t - 3))
                        else:
                            pe.wait_ge(*(z_done.at((1, 2)) if t == 1 else zst_out.at(1)))
                        pe.transpose(ps[:, 6 + (t - 1) % 2, 0:P], kn[:, (t - 1) % 2, :], ident[:]).then_inc(
                            *kT_full.tick(t - 1))
                for i in range(T + 3):
                    if i < T:
                        pe.wait_ge(*(vg_done.at(i - 2) if i >= 2 else yc_done.at((1, i))))
                        ins = rows_by_cols(ps[:, i % 2, 0:256], i, U_VG, list(range(KD)), 256)
                        if i < TS:
                            ins.then_inc(*vg_full.tick(i))
                    if i == 0:
                        pe.wait_ge(*kvu_done.at(TS))
                        for g in range(4):
                            ins = pe.transpose(ps[:, 4, g * P:(g + 1) * P], wnat[:, g, :], ident[:])
                        ins.then_inc(*prep_T.tick("ws"))
                        pe.wait_ge(*kvu_done.at(TS - 1))
                        for b in range(4):
                            ins = pe.transpose(ps[:, 5, b * P:(b + 1) * P], kc[:, b, :], ident[:])
                        ins.then_inc(*prep_T.tick("kc"))
                    if 2 <= i < T + 2:
                        spatial_mix(i - 2)
                    if i >= 3:
                        gated_turn(i - 3)
                for i in range(T + 4):
                    if 1 <= i <= T:
                        q_turn(i - 1)
                    if i < T:
                        pe.wait_ge(*(qn_raw.at(i - 1) if i >= 1 else vg_done.at(TS)))
                        ins = rows_by_cols(ps[:, 0, :], i, U_Q, list(range(KD)))
                        if i < TS:
                            ins.then_inc(*q_full.tick(i))
                    if 1 <= i <= T:
                        scores(i - 1)
                    if 3 <= i <= T + 2:
                        values(i - 3)
                    if 2 <= i <= T + 1:
                        if i == 2:
                            pe.wait_ge(*ygT_done.at(TS))
                        p_turn(i - 2)
                    if i >= 4:
                        group_sums(i - 4)
                    if i >= T:
                        project_out(0, i - T)
                for t in range(4, T):
                    project_out(0, t)
                for t in range(T + 2):
                    if t < T:
                        project_out(1, t)
                    if t == T:
                        pass
                    if t >= 2:
                        norm_turn(2, t - 2)
                pe.wait_ge(*out_acc.at(out_index(1, TS, 2)))
                pe.wait_ge(*norm_lo.at((2, TS - 1, 1)))
                pe.wait_ge(*norm_lo.at((2, TS, 1)))
                ff1(0)
                with pe.Fori(0, (FB - 2) // 2) as it:
                    for b in (1, 2):
                        ff1(b, it)
                        ff2(b - 1, it)
                ff1(FB - 1)
                ff2(FB - 2)
                ff2(FB - 1)


_INS = ["x_prompt", "x_sample", "cache_conv", "cache_k", "cache_v", "w_norm1", "w_in", "w_conv", "attn_sinks",
        "gmlp_ln_g", "gmlp_ln_b", "w_spatial", "b_spatial", "w_group_norm", "w_out", "w_norm2", "w_ff1", "w_ff2",
        "w_norm_final"]
_KV = (2, HD)
_OUTS = [(1, SEQ, D), (DEC_BATCH, DEC_SEQ, D), (DEPTH, 1, 2, 256), (DEPTH, 1, P) + _KV, (DEPTH, 1, P) + _KV,
         (DEPTH, DEC_BATCH, 2, 256), (DEPTH, DEC_BATCH, DEC_SEQ) + _KV, (DEPTH, DEC_BATCH, DEC_SEQ) + _KV,
         (DEPTH, DEC_BATCH, DEC_SEQ, 256)]


def rotary_tables():
    half = ROPE // 2
    inv = (np.float32(ROPE_THETA) ** (-np.arange(half, dtype=np.float32) * np.float32(2.0 / ROPE))).astype(np.float32)
    pos = np.concatenate([np.arange(SEQ), np.tile(PAST_LEN + np.arange(DEC_SEQ), DEC_BATCH)]).astype(np.float32)
    ang = (pos[:, None] * inv[None, :]).astype(np.float32).astype(np.float64)
    c, s = np.cos(ang).astype(np.float32), np.sin(ang).astype(np.float32)
    return [np.ascontiguousarray(np.concatenate(v, axis=1).reshape(T, P, ROPE).transpose(1, 0, 2))
            for v in ((c, c), (-s, s))]


def kernel(**inputs):
    import concourse.bacc as _bacc
    from concourse.bass_utils import run_bass_kernel_spmd as _run

    arrays = {f"in_{name}": np.ascontiguousarray(inputs[name]) for name in _INS}
    arrays["in_cos"], arrays["in_sin"] = rotary_tables()
    plan = {}
    for _ in range(2):
        plan["all"] = []
        nc = _bacc.Bacc("TRN2", target_bir_lowering=False, num_devices=1)
        args = [nc.dram_tensor(name, a.shape, mybir.dt.from_np(a.dtype), kind="ExternalInput").ap()
                for name, a in arrays.items()]
        args += [nc.dram_tensor(f"out_{i}", shape, F32, kind="ExternalOutput").ap() for i, shape in enumerate(_OUTS)]
        program(nc, args, plan)
        for s in plan["all"]:
            s.plan.update(s.seen, total=s.n)
    r = _run(nc, [arrays], core_ids=[0])
    return tuple(r.results[0][f"out_{i}"] for i in range(len(_OUTS)))
```

```python
from contextlib import ExitStack

import numpy as np

import concourse.bass as bass
from concourse import mybir

F32 = mybir.dt.float32
F32R = mybir.dt.float32r
ALU = mybir.AluOpType
ACT = mybir.ActivationFunctionType
AX_X = mybir.AxisListType.X

P = 128
D = 1024
SEQ = 1024
DEPTH = 2
DEC_BATCH = 8
DEC_SEQ = 16
PAST_LEN = 256
CHUNK = 64
HD = 64
HEADS = 8
G4 = 4
D_FF = 4096
ROPE = 16
ROPE_THETA = 500000.0
EPS = 1e-6
T = (SEQ + DEC_BATCH * DEC_SEQ) // P
TS = T - 1
ROWS = T * P
KD = D // P
GROUPS = 3
GW = ROWS // GROUPS
FB = 16
SC = HD ** -0.5
KEYS_S = CHUNK + DEC_SEQ
MASKED = -3.0e38

COL_CONV, COL_Q, COL_KVU, COL_VG = 0, 768, 1280, 1792
U_CONV, U_KVU, U_VG, U_Q, U_OUT, U_FF, U_END = 0, 16, 24, 32, 40, 56, 184
PAD_IDS = range(12, 16)
UNITS = U_END - len(PAD_IDS)
RAW = 4
Y_PER_LAYER = FB * T * 2
H_PER_LAYER = 2 * FB * GROUPS
Y_FULL_PER_LAYER = FB * TS * 2
H_FULL_PER_LAYER = 2 * FB * (GROUPS - 1)


def real(i):
    whole, i = divmod(i, U_END)
    return whole * UNITS + i - len([p for p in PAD_IDS if p < i])


class Signal:

    def __init__(self, nc, ctx, name, plan, now, by=1, primed=None):
        self.base = 0 if primed is None else 1
        self.sem = ctx.enter_context(nc.semaphore(name))
        self.plan = plan.setdefault(name, {})
        self.now, self.by, self.n, self.seen = now, by, 0, {}
        plan.setdefault("all", []).append(self)
        if primed is not None:
            primed.append(self.sem)

    def tick(self, key=None):
        self.n += self.by
        self.seen[key] = self.n
        return self.sem, self.by

    def at(self, key):
        n = self.plan.get(key, self.by)
        return self.sem, self.now["l"] * self.plan.get("total", self.by) + n + self.base

    def before(self, key):
        assert self.base
        return self.sem, self.now["l"] * self.plan.get(key, self.by) + self.base


class Primed:

    def __init__(self, nc, ctx, name, primed):
        self.sem = ctx.enter_context(nc.semaphore(name))
        primed.append(self.sem)

    def count(self, n):
        return self.sem, n + 1


def program(nc, io, plan):
    (x_prompt, x_sample, cache_conv, cache_k, cache_v, w_norm1, w_in, w_conv, sinks, ln_g, ln_b, w_spatial,
     b_spatial, w_group, w_out, w_norm2, w_ff1, w_ff2, w_final, cos_t, sin_t,
     y_prompt, y_sample, conv_p, k_p, v_p, conv_s, k_s, v_s, g_s) = io
    assert DEPTH == 2

    with ExitStack() as ctx:
        cursor = [16512]

        def place(name, shape, dt=F32, at=None):
            size = int(np.prod(shape[1:])) * 4
            if at is None:
                at = cursor[0]
                cursor[0] += (size + 15) // 16 * 16
            return nc.alloc_sbuf_tensor_at(name, shape, dt, offset=at, align_bytes=16)

        x = place("x", [P, T, D])
        hTh = place("hT_hi", [P, KD, ROWS], F32R)
        hTl = place("hT_lo", [P, KD, ROWS], F32R)
        base_u = cursor[0]
        ffh = place("ff_hi", [P, 4, ROWS], F32R)
        ffl = place("ff_lo", [P, 4, ROWS], F32R)
        u_sb = place("u_sb", [P, T, 256], at=base_u)
        kT = place("kT", [P, ROWS], at=base_u + 9216)
        v_sb = place("v_sb", [P, T, P], at=base_u + 13824)
        yc = place("yc", [P, 2, ROWS], at=base_u + 18432)
        base_c = base_u + 27648
        aT = place("aT", [P, ROWS], at=base_c)
        zT = place("zT", [P, 2 + SEQ + DEC_BATCH * (2 + DEC_SEQ)], at=base_c + 4608)
        qn = place("qn", [P, 512], at=base_c)
        qT = place("qT", [P, G4 * P], at=base_c + 2048)
        yat = place("yat", [P, G4, P], at=base_c + 4096)
        sq6 = place("sq6", [P, 6, P], at=base_c + 6144)
        cursor[0] = base_c + 9312
        wh = place("w_hi", [P, 8, 512], F32R)
        wl = place("w_lo", [P, 8, 512], F32R)
        raw = place("w_raw", [P, RAW, 512])
        base_n = cursor[0]
        xn = place("xn", [P, 2, D])
        gN = place("gN", [P, D])
        S = place("S", [P, 2, HEADS * P], at=base_n)
        pT = place("pT", [P, HEADS * P], at=base_n + 8192)
        wnat = place("wnat", [P, 4, P], at=base_n)
        kc = place("kc", [P, 4, P], at=base_n + 2048)
        ccin = place("ccin", [16, 256], at=base_n + 4096)
        cs_out = place("cs_out", [DEC_BATCH, 2, 256], at=base_n + 5120)
        cp_out = place("cp_out", [2, 256], at=base_n + 4096)
        gG = place("gG", [P, 256], at=base_n + 7168)
        kn = place("kn", [P, 2, P], at=base_n + 8192)
        vn = place("vn", [P, 2, 256], at=base_n + 9216)
        yg = place("yg", [P, 256], at=base_n + 11264)
        base_r = cursor[0]
        r_sb = place("r_sb", [P, 2, GW])
        r2_sb = place("r2_sb", [P, 2, GW])
        kcT = place("kcT", [P, 512], at=base_r)
        wsT = place("wsT", [P, 4, P], at=base_r + 2048)
        wsS = place("wsS", [P, 4, P], at=base_r + 4096)
        vs = place("vs", [KEYS_S, DEC_BATCH, P], at=base_r + 2048)
        squares = place("squares", [P, D], at=base_r)
        ident = place("ident", [P, P])
        cosb = place("cosb", [P, T, ROPE])
        sinb = place("sinb", [P, T, ROPE])
        base_l = cursor[0]
        lng = place("lng", [P, 256])
        lnb = place("lnb", [P, 256])
        ycg = place("ycg", [P, 2, P], at=base_l)
        vmix = place("vmix", [P, P], at=base_l + 1024)
        wcT = place("wcT", [P, 2, 3])
        gcT = place("gcT", [P, 6])
        bsp = place("bsp", [P, 2, 4])
        sink = place("sink", [P, 2, HEADS])
        sink1 = place("sink1", [P, 1])
        ccT = place("ccT", [P, 2, 16])
        ones = place("ones", [P, HEADS])
        nhalf = place("nhalf", [P, 4])
        rtA = place("rtA", [P, HEADS, ROPE])
        rtB = place("rtB", [P, HEADS, ROPE])
        ss = place("ss", [P, T])
        ms = place("ms", [P, T])
        rs = place("rs", [P, T])
        bst = place("bst", [P, 6])
        mv = place("mv", [P, 2, 2])
        ve = place("ve", [P, 2])
        rln = place("rln", [P, 2])
        ssG = place("ssG", [P, T])
        sg = place("sg", [P, T, 4])
        rG = place("rG", [P, T, 4])
        mx = place("mx", [P, HEADS])
        sd = place("sd", [P, HEADS])
        es = place("es", [P, HEADS])
        den = place("den", [P, HEADS])
        assert cursor[0] <= 229344, cursor[0]

        ps = ctx.enter_context(nc.psum_tensor("ps", [P, 8, 512], F32))

        now = {"l": 0}

        primed = []

        def sig(name, by=1, primed=None):
            return Signal(nc, ctx, name, plan, now, by, primed)

        def plain(name):
            return ctx.enter_context(nc.semaphore(name))

        x_in = [plain(f"x_in{t}") for t in range(T)]
        const_in = plain("const_in")
        ident_set = plain("ident_set")
        const_set = plain("const_set")
        raw_in = [plain(f"raw_in{s}") for s in range(RAW)]
        w_hi_done = plain("w_hi_done")
        w_ready = Primed(nc, ctx, "w_ready", primed)
        w_used = Primed(nc, ctx, "w_used", primed)
        h1_full = plain("h1_full")
        relu_done = Primed(nc, ctx, "relu_done", primed)
        r2_done = plain("r2_done")
        ffhi_done = plain("ffhi_done")
        ff_ready = plain("ff_ready")
        y_full = plain("y_full")
        x_added = Primed(nc, ctx, "x_added", primed)
        layer_in = sig("layer_in", 16)
        g1_in = sig("g1_in", 16)
        g2_in = sig("g2_in", 16)
        mid_in = sig("mid_in", 16)
        diag_in = sig("diag_in", 16)
        vs_in = sig("vs_in", 16)
        conv_sent = sig("conv_sent", 16)
        outs = sig("outs", 16)
        norm_ss, norm_ms, norm_r, xn_ready = sig("norm_ss"), sig("norm_ms"), sig("norm_r"), sig("xn_ready", primed=primed)
        norm_T, norm_hi, norm_lo = sig("norm_T", primed=primed), sig("norm_hi"), sig("norm_lo")
        conv_full, a_done, z_done, yc_done = sig("conv_full"), sig("a_done"), sig("z_done"), sig("yc_done")
        cc_T, cc_done, zst_T, zst_out = sig("cc_T"), sig("cc_done"), sig("zst_T"), sig("zst_out")
        kvu_full, kn_raw, kvu_done = sig("kvu_full"), sig("kn_raw"), sig("kvu_done")
        k_rot, kT_full, kT_done = sig("k_rot"), sig("kT_full"), sig("kT_done")
        prep_T, ws_done, kc_done, ws_zero = sig("prep_T"), sig("ws_done"), sig("kc_done"), sig("ws_zero")
        vg_full, vg_done, mv_done, ve_done, rln_done = (sig("vg_full"), sig("vg_done"), sig("mv_done"),
                                                        sig("ve_done"), sig("rln_done"))
        vn_ready, mixed_full, y_raw, ssg_done = sig("vn_ready"), sig("mixed_full"), sig("y_raw"), sig("ssg_done")
        yg_ready, ygT_full, ygT_done = sig("yg_ready"), sig("ygT_full"), sig("ygT_done")
        q_full, qn_raw, q_rot, qT_full, qT_done = (sig("q_full"), sig("qn_raw"), sig("q_rot"), sig("qT_full"),
                                                   sig("qT_done"))
        sc_full, s_sub, exp_done, p_ready = sig("sc_full"), sig("s_sub"), sig("exp_done"), sig("p_ready")
        pT_full, pT_done, vmix_set = sig("pT_full"), sig("pT_done"), sig("vmix_set")
        pv_full, yat_done, sq_done, mix_hi, mix_lo = (sig("pv_full"), sig("yat_done"), sig("sq_done"),
                                                      sig("mix_hi"), sig("mix_lo", primed=primed))
        ssm_full, sg_done, rg_done = sig("ssm_full"), sig("sg_done"), sig("rg_done")
        out_full, out_acc = sig("out_full"), sig("out_acc")
        dve_step = sig("dve_step")
        next_ss, next_ms, next_r = plain("next_ss"), plain("next_ms"), plain("next_r")
        fin_in, fin_y = plain("fin_in"), plain("fin_y")
        fin_out = [plain(f"fin_out{n}") for n in range(2)]

        block = ctx.enter_context(nc.Block())

        def tile(t):
            return slice(t * P, (t + 1) * P)

        def out_index(n, t, grp):
            return (n * T + t) * 3 + grp

        def y_count(b, t, n):
            return b * 2 * T + 2 * t + n + 1

        def h_count(c, g):
            return c * GROUPS + g + 1

        def slot_free(i, l):
            j = i - 8
            while j in PAD_IDS:
                j -= 8
            return l * real(j + 1 + U_END) if j < 0 else l * UNITS + real(j + 1)

        def released(i):
            return w_used.count(now["l"] * UNITS + real(i + 1))

        def first_splits(t):
            return {2: (0,), 3: (1,), 5: (2,), 7: (3,)}.get(t, ())

        def norm_banks(w, t):
            first = (0, 2)[t % 2] if w == 1 else (3, 5)[t % 2]
            return first, first + 1

        def ids_of_w1(b):
            return U_FF if b == 0 else U_FF + 4 + 8 * (b - 1)

        def ids_of_w2(b):
            return U_FF + 8 + 8 * b if b < FB - 1 else U_END - 4

        def load_x(engine, tiles):
            for t in tiles:
                src = x_prompt[0, tile(t), :] if t < TS else x_sample.rearrange("b s d -> (b s) d")
                engine.dma_start(x[:, t, :], src).then_inc(x_in[t], 16)

        @block.sync
        def _(sp):
            load_x(sp, (0, 1))

            in_rows = w_in.rearrange("l d e -> (l d) e")
            out_rows = w_out.rearrange("l d e -> (l d) e")
            ff2_rows = w_ff2.rearrange("l d e -> (l d) e")
            in_k = w_in.rearrange("l (k p) e -> (l k) p e", p=P)
            ff1_k = w_ff1.rearrange("l (k p) e -> (l k) p e", p=P)

            def load(dst, src, signal, key=None):
                sp.dma_start(dst, src, allow_slow_non_contiguous=True).then_inc(*signal.tick(key))

            def unit(n, shift, dst, src):
                l, s = now["l"], n % RAW
                if isinstance(shift, int) and n < RAW:
                    sp.wait_ge(*w_ready.count(l * (UNITS + n - RAW + 1)))
                else:
                    sp.wait_ge(*w_ready.count(l * UNITS + shift + (n - RAW + 1)))
                sp.dma_start(dst, src).then_inc(raw_in[s], 16)

            def rows_unit(n, shift, rows, r0, c0, cols):
                s = n % RAW
                unit(n, shift, raw[:, s, 0:cols], rows[bass.ds(r0, P), c0:c0 + cols])

            def cols_unit(n, shift, ks, k0, c0):
                s = n % RAW
                dst = raw[:, s, :].rearrange("p (k e) -> p k e", k=4)
                unit(n, shift, dst, ks[bass.ds(k0, 4), :, bass.ds(c0, P)].rearrange("k p e -> p k e"))

            def w1_units(n, shift, f0):
                for c in range(2):
                    for hk in range(2):
                        cols_unit(n + 2 * c + hk, shift, ff1_k, now["l"] * KD + 4 * hk, f0 + c * P)

            def w2_units(n, shift, f0):
                for nh in range(2):
                    for c in range(2):
                        rows_unit(n + 2 * nh + c, shift, ff2_rows, now["l"] * D_FF + f0 + c * P, nh * 512, 512)

            with sp.Fori(0, DEPTH) as l:
                now["l"] = l
                sp.wait_ge(*xn_ready.before((2, TS)))
                sp.nop(nofuse=True)
                load(gN[:], w_norm1[bass.ds(l, 1), :].broadcast_to([P, D]), g1_in)
                sp.wait_ge(*mix_lo.before(TS))
                sp.nop(nofuse=True)
                for c in range(2):
                    load(wcT[:, c, :], w_conv[l, :, c * P:(c + 1) * P].rearrange("j p -> p j"),
                         layer_in)
                    load(gcT[:, c:c + 1], w_group[bass.ds(l, 1), c * P:(c + 1) * P].rearrange("l p -> p l"), layer_in)
                for g in range(2):
                    load(gcT[64 * g:64 * g + 64, 2:6],
                         w_group[bass.ds(l, 1), 256 + 256 * g:512 + 256 * g].rearrange("l (h d) -> d (l h)", d=HD),
                         layer_in)
                load(lng[:], ln_g[bass.ds(l, 1), :].broadcast_to([P, 256]), layer_in)
                load(lnb[:], ln_b[bass.ds(l, 1), :].broadcast_to([P, 256]), layer_in)
                load(bsp[:, 0, :], b_spatial[l].rearrange("g p -> p g"), layer_in)
                load(sink[:, 0, :], sinks[bass.ds(l, 1), :].broadcast_to([P, HEADS]), layer_in)
                for b in range(DEC_BATCH):
                    load(bsp[16 * b:16 * b + 16, 1, :],
                         b_spatial[l, :, 0:16].rearrange("g p -> p g"), layer_in)
                    load(sink1[16 * b:16 * b + 16, :],
                         sinks[bass.ds(l, 1), b:b + 1].broadcast_to([16, 1]), layer_in, "last")
                for cb in range(6):
                    if cb == 4:
                        sp.wait_ge(*norm_T.at((1, TS)))
                        sp.nop(nofuse=True)
                        load(ccin[:], cache_conv[l].rearrange("b j c -> (b j) c"), mid_in)
                        load(gG[:], w_group[bass.ds(l, 1), 768:1024].broadcast_to([P, 256]), mid_in)
                        load(wnat[:], w_spatial[l].rearrange("g i j -> i g j"), mid_in)
                        for b in range(DEC_BATCH):
                            load(kc[64 * (b % 2):64 * (b % 2) + 64, b // 2, :],
                                 cache_k[l, b, CHUNK:2 * CHUNK].rearrange("r h d -> r (h d)"), mid_in, "last")
                    col = COL_CONV + (cb % 3) * 256 + (cb // 3) * P
                    for hk in range(2):
                        cols_unit(2 * cb + hk, 0, in_k, l * KD + 4 * hk, col)

                def in_units(first, col, cols):
                    for k in range(KD):
                        rows_unit(real(first + k), 0, in_rows, l * D + k * P, col, cols)

                in_units(U_KVU, COL_KVU, 512)
                in_units(U_VG, COL_VG, 256)
                sp.wait_ge(*ws_done.at("act"))
                sp.nop(nofuse=True)
                sp.wait_ge(*ws_zero.at(None))
                sp.nop(nofuse=True)
                for b in range(DEC_BATCH):
                    load(wsS[16 * b:16 * b + 16, :, 16 * b:16 * b + 16], wsT[0:16, :, 0:16], diag_in, "last")
                in_units(U_Q, COL_Q, 512)
                sp.wait_ge(*mixed_full.at(TS))
                sp.nop(nofuse=True)
                load(vs[0:64], cache_v[l, :, CHUNK:2 * CHUNK].rearrange("b r h d -> r b (h d)"),
                     vs_in)
                for b in range(DEC_BATCH):
                    load(vs[64:80, b, :], v_sb[16 * b:16 * b + 16, TS, :], vs_in, "last")
                for n in range(2):
                    for k in range(KD):
                        i = real(U_OUT + n * KD + k)
                        cols = slice(n * 512, n * 512 + 512)
                        if 2 <= k < 6:
                            src = w_out[bass.ds(l, 1), 256:768, cols].rearrange(
                                "l (g h d) e -> h (l g) d e", g=2, h=G4)[k - 2]
                        else:
                            src = out_rows[bass.ds(l * D + k * P, P), cols]
                        unit(i, 0, raw[:, i % RAW, :], src)
                w1_units(real(ids_of_w1(0)), 0, 0)
                with sp.Fori(0, FB - 1) as b:
                    w1_units(real(ids_of_w1(1)), b * 8, b * 256 + 256)
                    w2_units(real(ids_of_w2(0)), b * 8, b * 256)
                w2_units(real(ids_of_w2(FB - 1)), 0, (FB - 1) * 256)
            for t in range(T):
                dst = y_prompt[0, tile(t), :] if t < TS else y_sample.rearrange("b s d -> (b s) d")
                sp.wait_ge(fin_y, t + 1)
                sp.dma_start(dst, xn[:, t % 2, :]).then_inc(fin_out[t % 2], 16)
            sp.wait_ge(fin_out[0], 16 * ((T + 1) // 2))
            sp.wait_ge(fin_out[1], 16 * (T // 2))

        @block.gpsimd
        def _(pool):
            for sem in primed:
                pool.nop(nofuse=True).then_inc(sem, 1)
            nc.gpsimd.memset(ident[:], 0.0).then_inc(ident_set, 1)
            nc.gpsimd.memset(ones[:], 1.0).then_inc(const_set, 1)
            nc.gpsimd.memset(nhalf[:], -0.5).then_inc(const_set, 1)
            pool.wait_ge(ident_set, 1)
            nc.gpsimd.affine_select(out=ident[:], in_=ident[:], compare_op=ALU.not_equal, fill=1.0, base=0,
                                    pattern=[[-1, P]], channel_multiplier=1).then_inc(ident_set, 1)
            pool.dma_start(cosb[:], cos_t).then_inc(const_in, 16)
            pool.dma_start(sinb[:], sin_t).then_inc(const_in, 16)

            def here():
                pool.nop(nofuse=True)

            def load(dst, src, signal, key=None):
                pool.dma_start(dst, src).then_inc(*signal.tick(key))

            def powers():
                for t in range(T):
                    pool.wait_ge(*norm_ss.at(t))
                    here()
                    nc.gpsimd.tensor_scalar(ms[:, t:t + 1], ss[:, t:t + 1], 1.0 / D, EPS, ALU.mult,
                                            ALU.add).then_inc(*norm_ms.tick(t))
                    pool.wait_ge(*norm_ms.at(t))
                    nc.gpsimd.tensor_tensor(rs[:, t:t + 1], ms[:, t:t + 1], nhalf[:, 0:1],
                                            ALU.pow).then_inc(*norm_r.tick(t))

            def next_powers(layers):
                for t in range(T):
                    pool.wait_ge(next_ss, layers * T + t + 1)
                    here()
                    nc.gpsimd.tensor_scalar(ms[:, t:t + 1], ss[:, t:t + 1], 1.0 / D, EPS, ALU.mult,
                                            ALU.add).then_inc(next_ms, 1)
                    pool.wait_ge(next_ms, layers * T + t + 1)
                    nc.gpsimd.tensor_tensor(rs[:, t:t + 1], ms[:, t:t + 1], nhalf[:, 0:1], ALU.pow).then_inc(next_r, 1)

            next_powers(0)
            with pool.Fori(0, DEPTH) as l:
                now["l"] = l
                pool.wait_ge(*zst_out.at(1))
                here()
                load(conv_p[l].rearrange("b j c -> (b j) c"), cp_out[:], conv_sent)
                load(conv_s[l], cs_out[:], conv_sent, "last")
                for t, ko, vo in ((TS - 1, k_p, v_p), (TS, k_s, v_s)):
                    pool.wait_ge(*k_rot.at(t))
                    here()
                    load(ko[l].rearrange("b s h d -> (b s) (h d)"), kn[:, t % 2, :], outs)
                    pool.wait_ge(*kvu_done.at(t))
                    here()
                    load(vo[l].rearrange("b s h d -> (b s) (h d)"), v_sb[:, t, :], outs)
                for t in range(T):
                    pool.wait_ge(*mv_done.at(t))
                    here()
                    nc.gpsimd.tensor_scalar(ve[:, t % 2:t % 2 + 1], mv[:, t % 2, 1:2], 1.0, EPS, ALU.mult,
                                            ALU.add).then_inc(*ve_done.tick(t))
                    pool.wait_ge(*ve_done.at(t))
                    nc.gpsimd.tensor_tensor(rln[:, t % 2:t % 2 + 1], ve[:, t % 2:t % 2 + 1], nhalf[:, 0:1],
                                            ALU.pow).then_inc(*rln_done.tick(t))
                pool.wait_ge(*vn_ready.at(TS))
                here()
                load(g_s[l].rearrange("b s c -> (b s) c"), vn[:, TS % 2, :], outs, "last")
                for t in range(T):
                    pool.wait_ge(*sg_done.at(t))
                    nc.gpsimd.tensor_tensor(rG[:, t, 0:3], sg[:, t, 0:3], nhalf[:, 0:3],
                                            ALU.pow).then_inc(*rg_done.tick(t))
                pool.wait_ge(*pv_full.at(TS))
                here()
                load(gN[:], w_norm2[bass.ds(l, 1), :].broadcast_to([P, D]), g2_in)
                powers()
                next_powers(l + 1)
            now["l"] = DEPTH - 1
            pool.wait_ge(*xn_ready.at((2, TS)))
            pool.dma_start(gN[:], w_final.rearrange("(a d) -> a d", a=1).broadcast_to([P, D])).then_inc(fin_in, 16)
            pool.wait_ge(*conv_sent.at("last"))
            pool.wait_ge(*outs.at("last"))

        @block.scalar
        def _(act):
            def split(ids, cols=512):
                for i in ids:
                    l, n = now["l"], real(i)
                    act.wait_ge(raw_in[n % RAW], l * (16 * UNITS // RAW) + 16 * (n // RAW + 1))
                    act.wait_ge(*w_used.count(slot_free(i, l)))
                    nc.scalar.activation(wh[:, i % 8, 0:cols], raw[:, n % RAW, 0:cols],
                                         ACT.Copy).then_inc(w_hi_done, 1)

            def split_in_loop(i, it):
                l, n = now["l"], real(i)
                act.wait_ge(raw_in[n % RAW], l * (16 * UNITS // RAW) + it * (16 * 16 // RAW) + 16 * (n // RAW + 1))
                act.wait_ge(*w_used.count(l * UNITS + it * 16 + real(i - 7)))
                nc.scalar.activation(wh[:, i % 8, :], raw[:, n % RAW, :], ACT.Copy).then_inc(w_hi_done, 1)

            def norm_sum(t):
                act.wait_ge(*out_acc.at(out_index(1, t, 2)))
                if t >= 2:
                    act.wait_ge(*norm_T.at((2, t - 2)))
                else:
                    act.wait_ge(*pT_full.at(TS))
                nc.scalar.activation(xn[:, t % 2, :], x[:, t, :], ACT.Square,
                                     accum_out=ss[:, t:t + 1]).then_inc(*norm_ss.tick(t))

            def next_sums(layers):
                for t in range(T):
                    if isinstance(layers, int):
                        act.wait_ge(x_in[t], 16)
                        if t >= 1:
                            act.wait_ge(next_ss, t)
                    else:
                        act.wait_ge(*x_added.count(now["l"] * Y_PER_LAYER + y_count(FB - 1, t, 1)))
                        if t == 0:
                            act.wait_ge(ff_ready, (now["l"] + 1) * H_PER_LAYER)
                        act.wait_ge(next_ss, layers * T + t)
                    nc.scalar.activation(squares[:], x[:, t, :], ACT.Square,
                                         accum_out=ss[:, t:t + 1]).then_inc(next_ss, 1)

            def norm_high(w, t):
                for h, bank in enumerate(norm_banks(w, t)):
                    act.wait_ge(*norm_T.at((w, t)))
                    nc.scalar.activation(hTh[:, 4 * h:4 * h + 4, tile(t)],
                                         ps[:, bank, :].rearrange("p (k n) -> p k n", k=4),
                                         ACT.Copy).then_inc(*norm_hi.tick((w, t, h)))

            def relu_sq(c, it=0):
                l, bufs, banks = now["l"], c % 4, (3 * (c % 2), 3 * (c % 2) + 1, 3 * (c % 2) + 2)
                cnt = l * H_PER_LAYER + it * (4 * GROUPS)
                full = l * H_FULL_PER_LAYER + it * (4 * (GROUPS - 1))
                used = l * UNITS + it * 16
                for g in range(GROUPS + 1):
                    if g < GROUPS:
                        n = h_count(c, g)
                        if g < GROUPS - 1:
                            act.wait_ge(h1_full, full + c * (GROUPS - 1) + g + 1)
                        else:
                            act.wait_ge(*w_used.count(used + real(ids_of_w1(c // 2) + 2 * (c % 2) + 2)))
                        if n > 2:
                            act.wait_ge(r2_done, cnt + n - 2)
                            act.wait_ge(ffhi_done, cnt + n - 2)
                        nc.scalar.activation(r_sb[:, (n - 1) % 2, :], ps[:, banks[g], 0:GW],
                                             ACT.Relu).then_inc(relu_done.sem, 1)
                    if g >= 1:
                        n = h_count(c, g - 1)
                        act.wait_ge(*relu_done.count(cnt + n))
                        nc.scalar.activation(ffh[:, bufs, (g - 1) * GW:g * GW], r_sb[:, (n - 1) % 2, :],
                                             ACT.Square).then_inc(ffhi_done, 1)

            load_x(act, range(2, T))
            next_sums(0)
            with act.Fori(0, DEPTH) as l:
                now["l"] = l
                for t in range(T):
                    split(first_splits(t))
                    norm_high(1, t)
                split(range(4, 8))
                act.wait_ge(*cc_T.at(None))
                nc.scalar.activation(ccT[:], ps[:, 7, 0:32].rearrange("p (c n) -> p c n", c=2),
                                     ACT.Copy).then_inc(*cc_done.tick())

                def conv_a(c):
                    for g in range(GROUPS):
                        act.wait_ge(*(conv_full.at((3 * c, g)) if g < GROUPS - 1 else released(6 * c + 1)))
                        if c == 1:
                            act.wait_ge(*yc_done.at((0, GROUPS - 1)))
                        nc.scalar.activation(aT[:, g * GW:(g + 1) * GW], ps[:, (4, 0)[(3 * c) % 2] + g, 0:GW],
                                             ACT.Copy).then_inc(*a_done.tick((c, g)))

                def conv_state(c):
                    act.wait_ge(*zst_T.at(c))
                    nc.scalar.activation(cp_out[:, c * P:(c + 1) * P], ps[0:2, 7, 0:P], ACT.Copy).then_inc(
                        *zst_out.tick((c, 0)))
                    nc.scalar.activation(cs_out[:, :, c * P:(c + 1) * P],
                                         ps[0:DEC_BATCH, 7, P:3 * P].rearrange("b (j n) -> b j n", j=2), ACT.Copy).then_inc(
                        *zst_out.tick(c))

                conv_a(0)
                split(range(8, 12))
                conv_state(0)
                conv_a(1)
                split(range(U_KVU, U_KVU + 8))
                for t in range(T + 1):
                    if t < T:
                        if t == TS:
                            split(range(U_VG, U_VG + 4), 256)
                        act.wait_ge(*(kvu_full.at(t) if t < TS else released(U_KVU + 7)))
                        if t >= 2:
                            act.wait_ge(*kT_full.at(t - 2))
                        elif t == 0:
                            act.wait_ge(*xn_ready.at((1, TS)))
                        bank = ps[:, 4 + t % 2, :]
                        nc.scalar.activation(kn[:, t % 2, :], bank[:, 0:P], ACT.Copy).then_inc(*kn_raw.tick(t))
                        nc.scalar.activation(v_sb[:, t, :], bank[:, P:2 * P], ACT.Copy).then_inc(
                            *kvu_done.tick((t, "v")))
                        nc.scalar.activation(u_sb[:, t, :], bank[:, 2 * P:512], ACT.Gelu).then_inc(*kvu_done.tick(t))
                    if t == 1:
                        conv_state(1)
                    if t >= 1:
                        act.wait_ge(*kT_full.at(t - 1))
                        nc.scalar.activation(kT[:, tile(t - 1)], ps[:, 6 + (t - 1) % 2, 0:P],
                                             ACT.Copy).then_inc(*kT_done.tick(t - 1))
                    if t == TS:
                        split(range(U_VG + 4, U_VG + 8), 256)
                for i in range(T + 3):
                    if i < T:
                        if i == TS:
                            split(range(U_Q, U_Q + 4))
                        act.wait_ge(*(vg_full.at(i) if i < TS else released(U_VG + 7)))
                        if i >= 2:
                            act.wait_ge(*mixed_full.at(i - 2))
                        nc.scalar.activation(vn[:, i % 2, :], ps[:, i % 2, 0:256], ACT.Gelu).then_inc(
                            *vg_done.tick(i))
                    if i == 0:
                        act.wait_ge(*prep_T.at("ws"))
                        bank = ps[:, 4, :].rearrange("p (g n) -> p g n", g=4)
                        nc.scalar.activation(wsT[0:64], bank[0:64], ACT.Copy).then_inc(*ws_done.tick("a"))
                        nc.scalar.activation(wsT[64:128, :, 64:128], bank[64:128, :, 64:128],
                                             ACT.Copy).then_inc(*ws_done.tick("act"))
                        act.wait_ge(*prep_T.at("kc"))
                        nc.scalar.activation(kcT[:], ps[:, 5, :], ACT.Copy).then_inc(*kc_done.tick())
                    if 2 <= i < T + 2:
                        t = i - 2
                        act.wait_ge(*y_raw.at(t))
                        nc.scalar.activation(aT[:, 0:256], yg[:], ACT.Square,
                                             accum_out=ssG[:, t:t + 1]).then_inc(*ssg_done.tick(t))
                    if i == TS:
                        split(range(U_Q + 4, U_Q + 8))
                    if i >= 3:
                        t = i - 3
                        act.wait_ge(*ygT_full.at(t))
                        nc.scalar.activation(u_sb[:, t, :], ps[:, 6 + t % 2, 0:256], ACT.Copy).then_inc(
                            *ygT_done.tick(t))
                def copy_qT(t):
                    act.wait_ge(*qT_full.at(t))
                    if t >= 1:
                        act.wait_ge(*sc_full.at(t - 1))
                    src = ps[:, 2, :]
                    if t < TS:
                        nc.scalar.activation(qT[:], src, ACT.Copy).then_inc(*qT_done.tick(t))
                    else:
                        sv = src.rearrange("p (h b q) -> p b h q", h=G4, b=DEC_BATCH)
                        dv = qT[:].rearrange("p (b h q) -> p b h q", b=DEC_BATCH, h=G4)
                        nc.scalar.activation(dv, sv, ACT.Copy).then_inc(*qT_done.tick(t))

                for i in range(T + 4):
                    if 1 <= i < T:
                        copy_qT(i - 1)
                    if i < T:
                        if i == TS:
                            split(range(U_OUT, U_OUT + 4))
                        act.wait_ge(*(q_full.at(i) if i < TS else released(U_Q + 7)))
                        if i >= 1:
                            act.wait_ge(*qT_full.at(i - 1))
                        else:
                            act.wait_ge(*ssg_done.at(TS))
                        nc.scalar.activation(qn[:].rearrange("p (h g d) -> p g h d", h=G4, g=2),
                                             ps[:, 0, :].rearrange("p (g h d) -> p g h d", g=2, h=G4), ACT.Copy).then_inc(*qn_raw.tick(i))
                    if 1 <= i <= T:
                        t = i - 1
                        w = HEADS * P if t < TS else DEC_BATCH * KEYS_S
                        act.wait_ge(*s_sub.at(t))
                        nc.scalar.activation(S[:, t % 2, 0:w], S[:, t % 2, 0:w], ACT.Exp, scale=SC).then_inc(
                            *exp_done.tick((t, 0)))
                        nc.scalar.activation(es[:], sd[:], ACT.Exp, scale=SC).then_inc(*exp_done.tick(t))
                    if i == TS:
                        copy_qT(TS)
                        split(range(U_OUT + 4, U_OUT + 8))
                    if 3 <= i <= T + 2:
                        t = i - 3
                        act.wait_ge(*pv_full.at(t))
                        if t >= 1:
                            act.wait_ge(*ssm_full.at(t - 1))
                        nc.scalar.activation(sq6[:, 0:2, :], yc[:, :, tile(t)], ACT.Square).then_inc(
                            *sq_done.tick((t, 0)))
                        act.wait_ge(*yat_done.at(t))
                        nc.scalar.activation(sq6[:, 2:6, :], ps[:, 7, :].rearrange("p (h n) -> p h n", h=G4),
                                             ACT.Square).then_inc(*sq_done.tick(t))
                        act.wait_ge(*yat_done.at(t))
                        nc.scalar.activation(hTh[:, 0:2, tile(t)], ycg[:], ACT.Copy).then_inc(*mix_hi.tick((t, 0)))
                        nc.scalar.activation(hTh[:, 2:6, tile(t)], yat[:], ACT.Copy).then_inc(*mix_hi.tick((t, 1)))
                        nc.scalar.activation(hTh[:, 6:8, tile(t)],
                                             u_sb[:, t, :].rearrange("p (c n) -> p c n", c=2),
                                             ACT.Copy).then_inc(*mix_hi.tick(t))
                    if 2 <= i <= T + 1:
                        t = i - 2
                        act.wait_ge(*pT_full.at(t))
                        if t >= 1:
                            act.wait_ge(*pv_full.at(t - 1))
                        else:
                            act.wait_ge(*outs.at("last"))
                        n = P if t < TS else KEYS_S
                        nc.scalar.activation(pT[0:n, 0:512], ps[0:n, 5, :], ACT.Copy)
                        nc.scalar.activation(pT[0:n, 512:1024], ps[0:n, 6, :], ACT.Copy).then_inc(*pT_done.tick(t))
                split(range(U_OUT + 8, U_OUT + 16))
                for t in range(T + 2):
                    if t == TS:
                        split(range(U_FF, U_FF + 2))
                    if t < T:
                        norm_sum(t)
                    if t >= 2:
                        norm_high(2, t - 2)
                    if t == TS:
                        split(range(U_FF + 2, U_FF + 4))
                split(range(U_FF + 4, U_FF + 8))
                relu_sq(0)
                relu_sq(1)
                with act.Fori(0, (FB - 2) // 2) as it:
                    for b in (1, 2):
                        for i in range(ids_of_w2(b - 1), ids_of_w2(b - 1) + 4):
                            split_in_loop(i, it)
                        relu_sq(2 * b, it)
                        relu_sq(2 * b + 1, it)
                        for i in range(ids_of_w1(b + 1), ids_of_w1(b + 1) + 4):
                            split_in_loop(i, it)
                b = FB - 1
                split(range(ids_of_w2(b - 1), ids_of_w2(b - 1) + 4))
                relu_sq(2 * b)
                relu_sq(2 * b + 1)
                split(range(ids_of_w2(b), ids_of_w2(b) + 4))
                next_sums(l + 1)

        @block.vector
        def _(dve):
            def link(ins):
                ins.then_inc(*dve_step.tick(dve_step.n))
                dve.wait_ge(*dve_step.at(dve_step.n - 1))

            V = nc.vector

            def lo_unit(n, slot, count, cols=512):
                dve.wait_ge(w_hi_done, count)
                V.tensor_tensor(wl[:, slot, 0:cols], raw[:, n % RAW, 0:cols], wh[:, slot, 0:cols].bitcast(F32),
                                ALU.subtract).then_inc(w_ready.sem, 1)

            def split(ids, cols=512):
                for i in ids:
                    lo_unit(real(i), i % 8, now["l"] * UNITS + real(i) + 1, cols)

            def split_in_loop(i, it):
                lo_unit(real(i), i % 8, now["l"] * UNITS + it * 16 + real(i) + 1)

            def normalise(w, t):
                if w == 1:
                    dve.wait_ge(next_r, now["l"] * T + t + 1)
                    dve.wait_ge(*(norm_T.at((1, t - 2)) if t >= 2 else norm_T.before((2, TS))))
                else:
                    dve.wait_ge(*norm_r.at(t))
                dve.wait_ge(*(g1_in if w == 1 else g2_in).at(None))
                V.scalar_tensor_tensor(xn[:, t % 2, :], x[:, t, :], rs[:, t:t + 1], gN[:], ALU.mult,
                                       ALU.mult).then_inc(*xn_ready.tick((w, t)))

            def norm_low(w, t):
                for h, bank in enumerate(norm_banks(w, t)):
                    dve.wait_ge(*norm_hi.at((w, t, h)))
                    V.tensor_tensor(hTl[:, 4 * h:4 * h + 4, tile(t)],
                                    ps[:, bank, :].rearrange("p (k n) -> p k n", k=4),
                                    hTh[:, 4 * h:4 * h + 4, tile(t)].bitcast(F32),
                                    ALU.subtract).then_inc(*norm_lo.tick((w, t, h)))

            def rotate(src, heads, t, done):
                v = src.rearrange("p (h d) -> p h d", d=HD)
                c = cosb[:, t, :].unsqueeze(1).broadcast_to([P, heads, ROPE])
                s0 = sinb[:, t, 0:8].unsqueeze(1).broadcast_to([P, heads, 8])
                s1 = sinb[:, t, 8:16].unsqueeze(1).broadcast_to([P, heads, 8])
                V.tensor_tensor(rtA[:, 0:heads, :], v[:, :, 0:16], c, ALU.mult)
                V.tensor_tensor(rtB[:, 0:heads, 0:8], v[:, :, 8:16], s0, ALU.mult)
                link(V.tensor_tensor(rtB[:, 0:heads, 8:16], v[:, :, 0:8], s1, ALU.mult))
                V.tensor_tensor(v[:, :, 0:16], rtA[:, 0:heads, :], rtB[:, 0:heads, :], ALU.add).then_inc(*done.tick(t))
                dve.wait_ge(*done.at(t))

            zs = zT[:, 2 + SEQ:].rearrange("p (b n) -> p b n", b=DEC_BATCH)

            def conv_z(c):
                dve.wait_ge(*cc_done.at(None))
                if c == 0:
                    dve.wait_ge(*conv_full.at((1, 0)))
                    V.memset(zT[:, 0:2], 0.0)
                else:
                    dve.wait_ge(*zst_T.at(0))
                V.tensor_copy(zs[:, :, 0:2], ccT[:, c, :].rearrange("p (b j) -> p b j", j=2))
                for g in range(GROUPS):
                    cb = 3 * c + 1
                    bank = ps[:, (4, 0)[cb % 2] + g, :]
                    dve.wait_ge(*(conv_full.at((cb, g)) if g < GROUPS - 1 else released(2 * cb + 1)))
                    dve.wait_ge(*a_done.at((c, g)))
                    n = GW if g < GROUPS - 1 else SEQ - g * GW
                    last = V.tensor_tensor(zT[:, 2 + g * GW:2 + g * GW + n], bank[:, 0:n],
                                           aT[:, g * GW:g * GW + n], ALU.mult)
                    if g == GROUPS - 1:
                        last = V.tensor_tensor(zs[:, :, 2:], bank[:, n:GW].rearrange("p (b q) -> p b q", b=DEC_BATCH),
                                               aT[:, SEQ:].rearrange("p (b q) -> p b q", b=DEC_BATCH), ALU.mult)
                    last.then_inc(*z_done.tick((c, g)))

            def conv_taps(c):
                dve.wait_ge(*z_done.at((c, GROUPS - 1)))
                dve.wait_ge(*layer_in.at("last"))
                for zv, yv in ((lambda j: zT[:, j:j + SEQ], aT[:, 0:SEQ]),
                               (lambda j: zs[:, :, j:j + DEC_SEQ],
                                aT[:, SEQ:].rearrange("p (b q) -> p b q", b=DEC_BATCH))):
                    link(V.tensor_scalar(yv, zv(0), wcT[:, c, 0:1], None, ALU.mult))
                    for j in (1, 2):
                        link(V.scalar_tensor_tensor(yv, zv(j), wcT[:, c, j:j + 1], yv, ALU.mult, ALU.add))

            def conv_gate(c):
                for g in range(GROUPS):
                    cb = 3 * c + 2
                    dve.wait_ge(*(conv_full.at((cb, g)) if g < GROUPS - 1 else released(2 * cb + 1)))
                    V.tensor_tensor(yc[:, c, g * GW:(g + 1) * GW], ps[:, (4, 0)[cb % 2] + g, 0:GW],
                                    aT[:, g * GW:(g + 1) * GW], ALU.mult).then_inc(*yc_done.tick((c, g)))

            def scores_view(t):
                w = P if t < TS else KEYS_S
                return ps[:, 3:5, 0:4 * w].rearrange("p b (h n) -> p b h n", h=4), w

            def s_view(t, w):
                return S[:, t % 2, 0:8 * w].rearrange("p (b h n) -> p b h n", b=2, h=4)

            def by_head(v, w):
                return v.rearrange("p (b h) -> p b h", b=2).unsqueeze(3).broadcast_to([P, 2, 4, w])

            def softmax_max(t):
                v, w = scores_view(t)
                dve.wait_ge(*sc_full.at(t))
                if t == 0:
                    link(V.memset(ps[0:64, 3:5, :].rearrange("p b (h n) -> p (b h) n", h=4)[:, :, CHUNK:P], MASKED))
                kind = 0 if t < TS else 1
                link(V.tensor_reduce(mx[:].rearrange("p (b h) -> p b h", b=2), v, AX_X, ALU.max))
                link(V.tensor_tensor(mx[:], mx[:], sink[:, kind, :], ALU.max))
                if t >= 2:
                    dve.wait_ge(*pT_full.at(t - 2))
                elif t == 1:
                    dve.wait_ge(*conv_sent.at("last"))
                V.tensor_tensor(s_view(t, w), v, by_head(mx[:], w), ALU.subtract)
                V.tensor_tensor(sd[:], sink[:, kind, :], mx[:], ALU.subtract).then_inc(*s_sub.tick(t))

            def softmax_norm(t):
                w = P if t < TS else KEYS_S
                dve.wait_ge(*exp_done.at(t))
                link(V.tensor_reduce(den[:].rearrange("p (b h) -> p b h", b=2), s_view(t, w), AX_X, ALU.add))
                link(V.tensor_tensor(den[:], den[:], es[:], ALU.add))
                link(V.reciprocal(den[:], den[:]))
                V.tensor_tensor(s_view(t, w), s_view(t, w), by_head(den[:], w), ALU.mult).then_inc(*p_ready.tick(t))

            def mixed_rows(t):
                dve.wait_ge(*pv_full.at(t))
                if t >= 1:
                    dve.wait_ge(*mix_hi.at(t - 1))
                V.tensor_tensor(yat[:], ps[:, 7, :].rearrange("p (h n) -> p h n", h=G4),
                                gcT[:, 2:6].unsqueeze(2).broadcast_to([P, G4, P]), ALU.mult)
                V.tensor_tensor(ycg[:], yc[:, :, tile(t)], gcT[:, 0:2].unsqueeze(2).broadcast_to([P, 2, P]),
                                ALU.mult).then_inc(*yat_done.tick(t))

            def mixed_low(t):
                dve.wait_ge(*mix_hi.at(t))
                for k0, k1, src in ((0, 2, ycg[:]), (2, 6, yat[:]),
                                    (6, 8, u_sb[:, t, :].rearrange("p (c n) -> p c n", c=2))):
                    last = V.tensor_tensor(hTl[:, k0:k1, tile(t)], src, hTh[:, k0:k1, tile(t)].bitcast(F32),
                                           ALU.subtract)
                last.then_inc(*mix_lo.tick(t))

            def project_out(n, t):
                for grp in range(3):
                    q = out_index(n, t, grp)
                    unit = U_OUT + 8 * n + (1, 5, 7)[grp]
                    if n == 0 and t == TS:
                        split(range(U_OUT + 8 + (0, 2, 6)[grp], U_OUT + 8 + (2, 6, 8)[grp]))
                    dve.wait_ge(*(out_full.at(q) if t < TS else released(unit)))
                    dve.wait_ge(*rg_done.at(t))
                    if q >= 1:
                        dve.wait_ge(*out_acc.at(q - 1))
                    V.scalar_tensor_tensor(x[:, t, n * 512:n * 512 + 512], ps[:, (0, 2)[q % 2], :],
                                           rG[:, t, grp:grp + 1], x[:, t, n * 512:n * 512 + 512], ALU.mult,
                                           ALU.add).then_inc(*out_acc.tick(q))

            def square_low(c, it=0):
                cnt = now["l"] * H_PER_LAYER + it * (4 * GROUPS)
                for g in range(GROUPS + 1):
                    if g < GROUPS:
                        n = h_count(c, g)
                        dve.wait_ge(*relu_done.count(cnt + n))
                        if n > 2:
                            dve.wait_ge(ff_ready, cnt + n - 2)
                        V.tensor_tensor(r2_sb[:, (n - 1) % 2, :], r_sb[:, (n - 1) % 2, :], r_sb[:, (n - 1) % 2, :],
                                        ALU.mult).then_inc(r2_done, 1)
                    if g >= 1:
                        n = h_count(c, g - 1)
                        dve.wait_ge(ffhi_done, cnt + n)
                        dve.wait_ge(r2_done, cnt + n)
                        V.tensor_tensor(ffl[:, c % 4, (g - 1) * GW:g * GW], r2_sb[:, (n - 1) % 2, :],
                                        ffh[:, c % 4, (g - 1) * GW:g * GW].bitcast(F32),
                                        ALU.subtract).then_inc(ff_ready, 1)

            def add_ff2(b, it=0, ids=(), looped=False):
                l = now["l"]
                for t in range(T):
                    for n in range(2):
                        cnt = l * Y_PER_LAYER + it * (4 * T) + y_count(b, t, n)
                        if t < TS:
                            dve.wait_ge(y_full, l * Y_FULL_PER_LAYER + it * (4 * TS) + b * 2 * TS + 2 * t + n + 1)
                        else:
                            dve.wait_ge(*w_used.count(l * UNITS + it * 16 + real(ids_of_w2(b) + 2 * n + 2)))
                        if b >= 1:
                            dve.wait_ge(*x_added.count(cnt - 2 * T))
                        xv = x[:, t, n * 512:n * 512 + 512]
                        V.tensor_tensor(xv, ps[:, 6 + n, :], xv, ALU.add).then_inc(x_added.sem, 1)
                    if t < len(ids):
                        split_in_loop(ids[t], it) if looped else split([ids[t]])

            dve.wait_ge(const_in, 32)
            dve.wait_ge(const_set, 2)
            with dve.Fori(0, DEPTH) as l:
                now["l"] = l
                for t in range(T + 1):
                    if t < T:
                        normalise(1, t)
                    if t >= 1:
                        split(first_splits(t - 1))
                        norm_low(1, t - 1)
                split(range(4, 8))
                conv_z(0)
                split(range(8, 12))
                conv_taps(0)
                conv_gate(0)
                conv_z(1)
                conv_taps(1)
                split(range(U_KVU, U_KVU + 8))
                conv_gate(1)
                for t in range(T):
                    if t == TS:
                        split(range(U_VG, U_VG + 4), 256)
                    dve.wait_ge(*kn_raw.at(t))
                    rotate(kn[:, t % 2, :], 2, t, k_rot)
                split(range(U_VG + 4, U_VG + 8), 256)
                V.memset(wsT[64:128, :, 0:64], 0.0)
                V.memset(wsS[:], 0.0).then_inc(*ws_zero.tick())
                for i in range(T + 2):
                    if i < T:
                        if i == TS:
                            split(range(U_Q, U_Q + 4))
                        dve.wait_ge(*vg_done.at(i))
                        link(V.bn_stats(bst[:], vn[:, i % 2, :]))
                        dve.nop(nofuse=True)
                        V.bn_aggr(mv[:, i % 2, :], bst[:]).then_inc(*mv_done.tick(i))
                        dve.wait_ge(*mv_done.at(i))
                    if 1 <= i <= T:
                        t = i - 1
                        row = vn[:, t % 2, :]
                        dve.wait_ge(*rln_done.at(t))
                        link(V.tensor_scalar(row, row, mv[:, t % 2, 0:1], rln[:, t % 2:t % 2 + 1], ALU.subtract,
                                             ALU.mult))
                        link(V.tensor_tensor(row, row, lng[:], ALU.mult))
                        V.tensor_tensor(row, row, lnb[:], ALU.add).then_inc(*vn_ready.tick(t))
                    if i >= 2:
                        t = i - 2
                        kind = 0 if t < TS else 1
                        dve.wait_ge(*mixed_full.at(t))
                        if t >= 1:
                            dve.wait_ge(*ssg_done.at(t - 1))
                            dve.wait_ge(*yg_ready.at(t - 1))
                        link(V.tensor_tensor(yg[:].rearrange("p (g d) -> p g d", g=4),
                                             ps[:, 2 + t % 2, 0:256].rearrange("p (g d) -> p g d", g=4),
                                             bsp[:, kind, :].unsqueeze(2).broadcast_to([P, 4, HD]), ALU.add))
                        V.tensor_tensor(yg[:], yg[:], u_sb[:, t, :], ALU.mult).then_inc(*y_raw.tick(t))
                        dve.wait_ge(*y_raw.at(t))
                        V.tensor_tensor(u_sb[:, t, :], yg[:], gG[:], ALU.mult).then_inc(*yg_ready.tick(t))
                    if i == TS:
                        split(range(U_Q + 4, U_Q + 8))
                V.tensor_scalar(sink[:, 1, :], ones[:], sink1[:, 0:1], 8.0, ALU.mult, ALU.mult)
                link(V.tensor_scalar(sink[:, 0, :], sink[:, 0, :], 8.0, None, ALU.mult))
                for i in range(T + 4):
                    if i < T:
                        if i == TS:
                            split(range(U_OUT, U_OUT + 4))
                        dve.wait_ge(*qn_raw.at(i))
                        rotate(qn[:], HEADS, i, q_rot)
                    if 1 <= i <= T:
                        softmax_max(i - 1)
                    if i >= T:
                        project_out(0, 2 * (i - T))
                    if i == TS:
                        split(range(U_OUT + 4, U_OUT + 8))
                    if 3 <= i <= T + 2:
                        mixed_rows(i - 3)
                    if 2 <= i <= T:
                        t = i - 2
                        if t >= 1:
                            dve.wait_ge(*pv_full.at(t - 1))
                        if t < TS:
                            V.tensor_copy(vmix[0:64, :], v_sb[0:64, t, :])
                            if t == 0:
                                ins = V.memset(vmix[64:128, :], 0.0)
                            else:
                                ins = V.tensor_copy(vmix[64:128, :], v_sb[64:128, t - 1, :])
                            ins.then_inc(*vmix_set.tick(t))
                    if 1 <= i <= T:
                        softmax_norm(i - 1)
                    if 3 <= i <= T + 2:
                        mixed_low(i - 3)
                    if i >= 4:
                        t = i - 4
                        dve.wait_ge(*ssm_full.at(t))
                        V.tensor_scalar(sg[:, t, 0:1], ps[:, 1, 0:1], 1.0 / 256, EPS, ALU.mult, ALU.add)
                        V.tensor_scalar(sg[:, t, 1:2], ps[:, 1, 1:2], 1.0 / 512, EPS, ALU.mult, ALU.add)
                        V.tensor_scalar(sg[:, t, 2:3], ssG[:, t:t + 1], 1.0 / 256, EPS, ALU.mult,
                                        ALU.add).then_inc(*sg_done.tick(t))
                    if i >= T:
                        project_out(0, 2 * (i - T) + 1)
                project_out(0, TS)
                for t in range(T + 2):
                    if t == TS:
                        split(range(U_FF, U_FF + 2))
                    if t < T:
                        project_out(1, t)
                    if 1 <= t <= T:
                        normalise(2, t - 1)
                    if t >= 2:
                        norm_low(2, t - 2)
                    if t == TS:
                        split(range(U_FF + 2, U_FF + 4))
                split(range(U_FF + 4, U_FF + 8))
                square_low(0)
                square_low(1)

                def block_of_ff(b, it=0, looped=False, ids=()):
                    for i in range(ids_of_w2(b - 1), ids_of_w2(b - 1) + 4):
                        split_in_loop(i, it) if looped else split([i])
                    square_low(2 * b, it)
                    square_low(2 * b + 1, it)
                    add_ff2(b - 1, it, ids, looped)

                dve.wait_ge(*out_acc.at(out_index(1, TS, 2)))
                dve.nop(nofuse=True)
                with dve.Fori(0, (FB - 2) // 2) as it:
                    for b in (1, 2):
                        block_of_ff(b, it, True, range(ids_of_w1(b + 1), ids_of_w1(b + 1) + 4))
                block_of_ff(FB - 1, ids=range(ids_of_w2(FB - 1), ids_of_w2(FB - 1) + 4))
                add_ff2(FB - 1)
            dve.wait_ge(fin_in, 16)
            for t in range(T):
                dve.wait_ge(next_r, DEPTH * T + t + 1)
                if t >= 2:
                    dve.wait_ge(fin_out[t % 2], 16 * (t // 2))
                V.scalar_tensor_tensor(xn[:, t % 2, :], x[:, t, :], rs[:, t:t + 1], gN[:], ALU.mult,
                                       ALU.mult).then_inc(fin_y, 1)

        @block.tensor
        def _(pe):
            def product(out, sh, sl, mh, ml, first, last):
                pe.matmul(out, sh, mh, start=first, stop=False)
                pe.matmul(out, sh, ml, start=False, stop=False)
                return pe.matmul(out, sl, mh, start=False, stop=last)

            def unit_ready(i):
                pe.wait_ge(*w_ready.count(now["l"] * UNITS + real(i) + 1))

            def rows_by_cols(out, t, first_id, ks, cols=512, sum_of=None):
                sum_of = sum_of or ks
                for k in ks:
                    if t == 0:
                        unit_ready(first_id + k)
                    s = (first_id + k) % 8
                    ins = product(out, hTh[:, k, tile(t)], hTl[:, k, tile(t)], wh[:, s, 0:cols], wl[:, s, 0:cols],
                                  k == sum_of[0], k == sum_of[-1])
                    if t == TS:
                        ins.then_inc(w_used.sem, 1)
                return ins

            def cols_by_rows(out, g, first_id, it=0, ks=range(KD)):
                for k in ks:
                    i = first_id + k // 4
                    if g == 0 and k % 4 == 0:
                        pe.wait_ge(*w_ready.count(now["l"] * UNITS + it * 16 + real(i) + 1))
                    w0 = (k % 4) * P
                    ins = product(out, wh[:, i % 8, w0:w0 + P], wl[:, i % 8, w0:w0 + P],
                                  hTh[:, k, g * GW:(g + 1) * GW], hTl[:, k, g * GW:(g + 1) * GW],
                                  k == 0, k == KD - 1)
                    if g == GROUPS - 1 and k % 4 == 3:
                        ins.then_inc(w_used.sem, 1)
                return ins

            def norm_turn(w, t):
                pe.wait_ge(*xn_ready.at((w, t)))
                if t >= 2:
                    pe.wait_ge(*norm_lo.at((w, t - 2, 1)))
                for k in range(KD):
                    bank = norm_banks(w, t)[k // 4]
                    ins = pe.transpose(ps[:, bank, (k % 4) * P:(k % 4 + 1) * P], xn[:, t % 2, tile(k)], ident[:])
                ins.then_inc(*norm_T.tick((w, t)))

            def conv_cols(cb, g, ks=range(KD)):
                if ks[0] == 0 and cb >= 2:
                    c, kind = divmod(cb - 2, 3)
                    pe.wait_ge(*(a_done, z_done, yc_done)[kind].at((c, g)))
                elif ks[0] == 0 and cb == 1:
                    pe.wait_ge(*norm_lo.at((1, TS, 1)))
                    pe.wait_ge(*norm_lo.at((1, TS - 1, 1)))
                elif ks[0] == 0:
                    pe.wait_ge(*norm_lo.at((1, 3 * g + 2, 1)))
                ins = cols_by_rows(ps[:, (4, 0)[cb % 2] + g, 0:GW], g, 2 * cb, ks=ks)
                if g < GROUPS - 1 and ks[-1] == KD - 1:
                    ins.then_inc(*conv_full.tick((cb, g)))

            def conv_state(c):
                pe.wait_ge(*z_done.at((c, GROUPS - 1)))
                if c == 0:
                    pe.wait_ge(*cc_done.at(None))
                else:
                    pe.wait_ge(*zst_out.at(0))
                pe.transpose(ps[0:2, 7, 0:P], zT[:, SEQ:SEQ + 2], ident[:])
                z_streams = zT[:, 2 + SEQ:].rearrange("p (b n) -> p b n", b=DEC_BATCH)
                for j in range(2):
                    ins = pe.transpose(ps[0:DEC_BATCH, 7, (1 + j) * P:(2 + j) * P], z_streams[:, :, DEC_SEQ + j],
                                       ident[:])
                ins.then_inc(*zst_T.tick(c))

            def spatial_mix(t):
                w = wsT if t < TS else wsS
                if t == 0:
                    pe.wait_ge(*ws_done.at("act"))
                    pe.wait_ge(*ws_zero.at(None))
                    pe.wait_ge(*yc_done.at((1, 2)))
                if t == TS:
                    pe.wait_ge(*diag_in.at("last"))
                pe.wait_ge(*vn_ready.at(t))
                if t >= 2:
                    pe.wait_ge(*yg_ready.at(t - 2))
                for g in range(4):
                    ins = pe.matmul(ps[:, 2 + t % 2, g * HD:(g + 1) * HD], w[:, g, :], vn[:, t % 2, g * HD:(g + 1) * HD],
                                    start=True, stop=True)
                ins.then_inc(*mixed_full.tick(t))

            def gated_turn(t):
                pe.wait_ge(*yg_ready.at(t))
                pe.wait_ge(*(ygT_done.at(t - 2) if t >= 2 else kT_done.at(TS - t)))
                pe.transpose(ps[:, 6 + t % 2, 0:P], u_sb[:, t, 0:P], ident[:])
                pe.transpose(ps[:, 6 + t % 2, P:2 * P], u_sb[:, t, P:2 * P], ident[:]).then_inc(*ygT_full.tick(t))

            def q_turn(t):
                pe.wait_ge(*q_rot.at(t))
                if t >= 1:
                    pe.wait_ge(*qT_done.at(t - 1))
                for h in range(G4):
                    ins = pe.transpose(ps[:, 2, h * P:(h + 1) * P], qn[:, h * P:(h + 1) * P], ident[:])
                ins.then_inc(*qT_full.tick(t))

            def scores(t):
                pe.wait_ge(*qT_done.at(t))
                if t >= 1:
                    pe.wait_ge(*s_sub.at(t - 1))
                else:
                    pe.wait_ge(*kT_done.at(TS))
                    pe.wait_ge(*kc_done.at(None))
                pe.nop(nofuse=True)
                k0 = t * P
                for g in range(2):
                    rows = slice(64 * g, 64 * g + 64)
                    bank = ps[:, 3 + g, :]
                    for h in range(G4):
                        if t == TS:
                            break
                        c0 = h * P
                        qh = qT[rows, h * P:(h + 1) * P]
                        pe.matmul(bank[0:64, c0:c0 + 64], qh[:, 0:64], kT[rows, k0:k0 + 64], start=True, stop=True)
                        if t > 0:
                            pe.matmul(bank[0:64, c0 + 64:c0 + P], qh[:, 0:64], kT[rows, k0 - 64:k0], start=True,
                                      stop=True)
                        ins = pe.matmul(bank[64:128, c0:c0 + P], qh[:, 64:128], kT[rows, k0:k0 + P], start=True,
                                        stop=True)
                if t == TS:
                    for b in range(DEC_BATCH):
                        bank = ps[:, 3 + b // 4, (b % 4) * KEYS_S:(b % 4 + 1) * KEYS_S]
                        for g in range(2):
                            rows = slice(64 * g, 64 * g + 64)
                            qb = qT[rows, b * 64:(b + 1) * 64]
                            pe.matmul(bank[rows, 0:64], qb, kcT[rows, b * 64:(b + 1) * 64], start=True, stop=True)
                            ins = pe.matmul(bank[rows, 64:80], qb, kT[rows, k0 + 16 * b:k0 + 16 * b + 16],
                                            start=True, stop=True)
                ins.then_inc(*sc_full.tick(t))

            def p_turn(t):
                pe.wait_ge(*p_ready.at(t))
                if t >= 1:
                    pe.wait_ge(*pT_done.at(t - 1))
                n = P if t < TS else KEYS_S
                for h in range(HEADS):
                    ins = pe.transpose(ps[0:n, 5 + h // 4, (h % 4) * P:(h % 4 + 1) * P],
                                       S[:, t % 2, h * n:(h + 1) * n], ident[:])
                ins.then_inc(*pT_full.tick(t))

            def values(t):
                pe.wait_ge(*pT_done.at(t))
                if t < TS:
                    pe.wait_ge(*vmix_set.at(t))
                if t >= 1:
                    pe.wait_ge(*sq_done.at(t - 1))
                else:
                    pe.wait_ge(*ygT_done.at(TS - 1))
                out = ps[:, 7, :].rearrange("p (h n) -> p h n", h=G4)
                pv = pT[:].rearrange("p (g h n) -> p g h n", g=2, h=G4)
                if t < TS:
                    for g in range(2):
                        rows = slice(64 * g, 64 * g + 64)
                        for half, vv in enumerate((vmix[:, rows], v_sb[:, t, rows])):
                            q = slice(64 * half, 64 * half + 64)
                            ins = pe.matmul(out[rows, :, q], vv, pv[:, g, :, q], start=True, stop=True)
                else:
                    pe.wait_ge(*vs_in.at("last"))
                    for b in range(DEC_BATCH):
                        for g in range(2):
                            rows = slice(64 * g, 64 * g + 64)
                            ins = pe.matmul(out[rows, :, 16 * b:16 * b + 16], vs[0:KEYS_S, b, rows],
                                            pT[0:KEYS_S, b * P + 64 * g:b * P + 64 * g + 64], start=True, stop=True)
                ins.then_inc(*pv_full.tick(t))

            def group_sums(t):
                pe.wait_ge(*sq_done.at(t))
                if t >= 1:
                    pe.wait_ge(*sg_done.at(t - 1))
                for col, ks in ((0, range(0, 2)), (1, range(2, 6))):
                    for k in ks:
                        ins = pe.matmul(ps[:, 1, col:col + 1], sq6[:, k, :], ones[:, 0:1], start=k == ks[0],
                                        stop=k == ks[-1])
                ins.then_inc(*ssm_full.tick(t))

            def project_out(n, t):
                for grp, ks in enumerate((range(0, 2), range(2, 6), range(6, 8))):
                    q = out_index(n, t, grp)
                    if grp == 0 and n == 0:
                        pe.wait_ge(*mix_lo.at(t))
                    if q >= 2:
                        pe.wait_ge(*out_acc.at(q - 2))
                    else:
                        pe.wait_ge(*(qn_raw, qT_done)[q].at(TS))
                    ins = rows_by_cols(ps[:, (0, 2)[q % 2], :], t, U_OUT + 8 * n, list(ks))
                    if t < TS:
                        ins.then_inc(*out_full.tick(q))

            def ff1(b, it=0, groups=range(GROUPS), chunks=(0, 1)):
                l = now["l"]
                for cc in chunks:
                    c = 2 * b + cc
                    for g in groups:
                        if c >= 2:
                            pe.wait_ge(*relu_done.count(l * H_PER_LAYER + it * (4 * GROUPS) + h_count(c - 2, g)))
                        ins = cols_by_rows(ps[:, 3 * cc + g, 0:GW], g, ids_of_w1(b) + 2 * cc, it)
                        if g < GROUPS - 1:
                            ins.then_inc(h1_full, 1)

            def ff2(b, it=0):
                l = now["l"]
                for t in range(T):
                    if t % 3 == 0:
                        pe.wait_ge(ff_ready, l * H_PER_LAYER + it * (4 * GROUPS) + h_count(2 * b + 1, t // 3))
                    for n in range(2):
                        if b > 0 or t > 0:
                            pe.wait_ge(*x_added.count(l * Y_PER_LAYER + it * (4 * T) + y_count(b, t, n) - 2))
                        for cc in range(2):
                            i = ids_of_w2(b) + 2 * n + cc
                            if t == 0:
                                pe.wait_ge(*w_ready.count(l * UNITS + it * 16 + real(i) + 1))
                            ch = (2 * b + cc) % 4
                            ins = product(ps[:, 6 + n, :], ffh[:, ch, tile(t)], ffl[:, ch, tile(t)], wh[:, i % 8, :],
                                          wl[:, i % 8, :], cc == 0, cc == 1)
                            if t == TS:
                                ins.then_inc(w_used.sem, 1)
                        if t < TS:
                            ins.then_inc(y_full, 1)

            pe.wait_ge(ident_set, 2)
            pe.wait_ge(const_set, 2)
            with pe.Fori(0, DEPTH) as l:
                now["l"] = l
                pe.wait_ge(*relu_done.count(l * H_PER_LAYER))
                pe.wait_ge(*x_added.count(l * Y_PER_LAYER))
                for t in range(T + 5):
                    if t < T:
                        norm_turn(1, t)
                    if 4 <= t < 13:
                        g, third = divmod(t - 4, 3)
                        conv_cols(0, g, (range(0, 3), range(3, 6), range(6, 8))[third])
                pe.wait_ge(*mid_in.at("last"))
                pe.nop(nofuse=True)
                for c in range(2):
                    ins = pe.transpose(ps[:, 7, 16 * c:16 * c + 16], ccin[0:16, c * P:(c + 1) * P], ident[0:16, 0:16])
                ins.then_inc(*cc_T.tick())
                for cb in range(1, 6):
                    for g in range(GROUPS):
                        conv_cols(cb, g)
                    if cb == 2:
                        conv_state(0)
                for t in range(T + 1):
                    if t < T:
                        pe.wait_ge(*(kvu_done.at(t - 2) if t >= 2 else z_done.at((1, t))))
                        ins = rows_by_cols(ps[:, 4 + t % 2, :], t, U_KVU, list(range(KD)))
                        if t < TS:
                            ins.then_inc(*kvu_full.tick(t))
                    if t == 1:
                        conv_state(1)
                    if t >= 1:
                        pe.wait_ge(*k_rot.at(t - 1))
                        if t - 1 >= 2:
                            pe.wait_ge(*kT_done.at(t - 3))
                        else:
                            pe.wait_ge(*(z_done.at((1, 2)) if t == 1 else zst_out.at(1)))
                        pe.transpose(ps[:, 6 + (t - 1) % 2, 0:P], kn[:, (t - 1) % 2, :], ident[:]).then_inc(
                            *kT_full.tick(t - 1))
                for i in range(T + 3):
                    if i < T:
                        pe.wait_ge(*(vg_done.at(i - 2) if i >= 2 else yc_done.at((1, i))))
                        ins = rows_by_cols(ps[:, i % 2, 0:256], i, U_VG, list(range(KD)), 256)
                        if i < TS:
                            ins.then_inc(*vg_full.tick(i))
                    if i == 0:
                        pe.wait_ge(*kvu_done.at(TS))
                        for g in range(4):
                            ins = pe.transpose(ps[:, 4, g * P:(g + 1) * P], wnat[:, g, :], ident[:])
                        ins.then_inc(*prep_T.tick("ws"))
                        pe.wait_ge(*kvu_done.at(TS - 1))
                        for b in range(4):
                            ins = pe.transpose(ps[:, 5, b * P:(b + 1) * P], kc[:, b, :], ident[:])
                        ins.then_inc(*prep_T.tick("kc"))
                    if 2 <= i < T + 2:
                        spatial_mix(i - 2)
                    if i >= 3:
                        gated_turn(i - 3)
                    if i in (TS, T):
                        if i == TS:
                            pe.wait_ge(*vg_done.at(TS))
                        half = range(0, KD // 2) if i == TS else range(KD // 2, KD)
                        ins = rows_by_cols(ps[:, 0, :], 0, U_Q, half, sum_of=range(KD))
                        if i == T:
                            ins.then_inc(*q_full.tick(0))
                for i in range(T + 4):
                    if 1 <= i <= T:
                        q_turn(i - 1)
                    if 1 <= i < T:
                        pe.wait_ge(*qn_raw.at(i - 1))
                        ins = rows_by_cols(ps[:, 0, :], i, U_Q, list(range(KD)))
                        if i < TS:
                            ins.then_inc(*q_full.tick(i))
                    if 1 <= i <= T:
                        scores(i - 1)
                    if i >= T:
                        project_out(0, 2 * (i - T))
                    if 3 <= i <= T + 2:
                        values(i - 3)
                    if 2 <= i <= T + 1:
                        if i == 2:
                            pe.wait_ge(*ygT_done.at(TS))
                        p_turn(i - 2)
                    if i >= 4:
                        group_sums(i - 4)
                    if i >= T:
                        project_out(0, 2 * (i - T) + 1)
                project_out(0, TS)
                for t in range(T + 2):
                    if t < T:
                        project_out(1, t)
                    if t >= T:
                        g = t - T
                        pe.wait_ge(*out_acc.at(out_index(1, TS, 2)))
                        pe.wait_ge(*norm_lo.at((2, 3 * g + 2, 1)))
                        ff1(0, groups=(g,), chunks=(0,))
                    if t >= 2:
                        norm_turn(2, t - 2)
                pe.wait_ge(*norm_lo.at((2, TS - 1, 1)))
                pe.wait_ge(*norm_lo.at((2, TS, 1)))
                ff1(0, groups=(2,), chunks=(0,))
                ff1(0, chunks=(1,))
                with pe.Fori(0, (FB - 2) // 2) as it:
                    for b in (1, 2):
                        ff1(b, it)
                        ff2(b - 1, it)
                ff1(FB - 1)
                ff2(FB - 2)
                ff2(FB - 1)


_INS = ["x_prompt", "x_sample", "cache_conv", "cache_k", "cache_v", "w_norm1", "w_in", "w_conv", "attn_sinks",
        "gmlp_ln_g", "gmlp_ln_b", "w_spatial", "b_spatial", "w_group_norm", "w_out", "w_norm2", "w_ff1", "w_ff2",
        "w_norm_final"]
_KV = (2, HD)
_OUTS = [(1, SEQ, D), (DEC_BATCH, DEC_SEQ, D), (DEPTH, 1, 2, 256), (DEPTH, 1, P) + _KV, (DEPTH, 1, P) + _KV,
         (DEPTH, DEC_BATCH, 2, 256), (DEPTH, DEC_BATCH, DEC_SEQ) + _KV, (DEPTH, DEC_BATCH, DEC_SEQ) + _KV,
         (DEPTH, DEC_BATCH, DEC_SEQ, 256)]


def rotary_tables():
    half = ROPE // 2
    inv = (np.float32(ROPE_THETA) ** (-np.arange(half, dtype=np.float32) * np.float32(2.0 / ROPE))).astype(np.float32)
    pos = np.concatenate([np.arange(SEQ), np.tile(PAST_LEN + np.arange(DEC_SEQ), DEC_BATCH)]).astype(np.float32)
    ang = (pos[:, None] * inv[None, :]).astype(np.float32).astype(np.float64)
    c, s = np.cos(ang).astype(np.float32), np.sin(ang).astype(np.float32)
    return [np.ascontiguousarray(np.concatenate(v, axis=1).reshape(T, P, ROPE).transpose(1, 0, 2))
            for v in ((c, c), (-s, s))]


def kernel(**inputs):
    import concourse.bacc as _bacc
    from concourse.bass_utils import run_bass_kernel_spmd as _run

    arrays = {f"in_{name}": np.ascontiguousarray(inputs[name]) for name in _INS}
    arrays["in_cos"], arrays["in_sin"] = rotary_tables()
    plan = {}
    for _ in range(2):
        plan["all"] = []
        nc = _bacc.Bacc("TRN2", target_bir_lowering=False, num_devices=1)
        args = [nc.dram_tensor(name, a.shape, mybir.dt.from_np(a.dtype), kind="ExternalInput").ap()
                for name, a in arrays.items()]
        args += [nc.dram_tensor(f"out_{i}", shape, F32, kind="ExternalOutput").ap() for i, shape in enumerate(_OUTS)]
        program(nc, args, plan)
        for s in plan["all"]:
            s.plan.update(s.seen, total=s.n)
    r = _run(nc, [arrays], core_ids=[0])
    return tuple(r.results[0][f"out_{i}"] for i in range(len(_OUTS)))
```
